# Optimizing a Trainium2 kernel written in Bass

```python
import jax, jax.numpy as jnp
from jax import lax
import numpy as np

D_MODEL = 2048
BATCH = 1
SEQ = 512
DEPTH = 1

GLA_HEADS = 4
GLA_DK = 128
GLA_DV = 256
GLA_RANK = 16
GLA_GATE_NORM = 16.0
GLA_CHUNK = 64
SWA_HEADS = 16
SWA_KV_HEADS = 2
SWA_HEAD_DIM = 64
WINDOW = 128
ROPE_THETA = 10000.0
D_FF = 5632
CONV_WIDTH = 3
EPS = 1e-6
NEG_INF = -1e30

GLA_QK_W = GLA_HEADS * GLA_DK
GLA_V_W = GLA_HEADS * GLA_DV
SWA_Q_W = SWA_HEADS * SWA_HEAD_DIM
SWA_KV_W = SWA_KV_HEADS * SWA_HEAD_DIM
MIX_WIDTH = GLA_V_W + SWA_Q_W
IN_SPLITS = (GLA_QK_W, GLA_QK_W, GLA_V_W, GLA_V_W, GLA_RANK, SWA_Q_W, SWA_KV_W, SWA_KV_W)
IN_WIDTH = GLA_QK_W * 2 + GLA_V_W * 2 + GLA_RANK + SWA_Q_W + SWA_KV_W * 2

kernel_name = "hymba_gla_swa_sink_convffn"

def rms_norm(x, g):
    xf = x.astype(jnp.float32)
    y = xf * lax.rsqrt(jnp.mean(xf * xf, axis=-1, keepdims=True) + EPS)
    return (y * g.astype(jnp.float32)).astype(x.dtype)

def split_cols(proj):
    outs = []
    start = 0
    for w in IN_SPLITS:
        outs.append(proj[..., start:start + w])
        start += w
    return outs

def rope(t, positions):
    half = t.shape[-1] // 2
    inv_freq = ROPE_THETA ** (-jnp.arange(half, dtype=jnp.float32) / half)
    ang = positions.astype(jnp.float32)[..., None] * inv_freq
    cos = jnp.cos(ang)[:, :, None, :]
    sin = jnp.sin(ang)[:, :, None, :]
    tf = t.astype(jnp.float32)
    t1, t2 = tf[..., :half], tf[..., half:]
    return jnp.concatenate([t1 * cos - t2 * sin, t2 * cos + t1 * sin], axis=-1).astype(t.dtype)

def gla_group(q, k, v, g_out, a_low, w_a_up, b_a_up, gn_gain):
    B, S, _ = q.shape
    C = GLA_CHUNK
    N = S // C
    f32 = jnp.float32
    log_a = jax.nn.log_sigmoid((a_low.astype(f32) @ w_a_up.astype(f32)) + b_a_up.astype(f32)) / GLA_GATE_NORM

    def to_chunks(t, d):
        return t.astype(f32).reshape(B, N, C, GLA_HEADS, d).transpose(0, 3, 1, 2, 4)

    qc = to_chunks(q, GLA_DK) * (GLA_DK ** -0.5)
    kc = to_chunks(k, GLA_DK)
    vc = to_chunks(v, GLA_DV)
    bcum = jnp.cumsum(to_chunks(log_a, GLA_DK), axis=3)
    b_last = bcum[:, :, :, -1:, :]
    q_e = qc * jnp.exp(bcum)
    k_e = kc * jnp.exp(-bcum)
    k_d = kc * jnp.exp(b_last - bcum)

    causal = jnp.tril(jnp.ones((C, C), dtype=bool))
    scores = jnp.where(causal, jnp.einsum('bhnid,bhnjd->bhnij', q_e, k_e), 0.0)
    o_intra = jnp.einsum('bhnij,bhnjv->bhniv', scores, vc)

    decay = jnp.exp(b_last[:, :, :, 0, :])
    kv = jnp.einsum('bhncd,bhncv->bhndv', k_d, vc)

    def step(state, inp):
        dec, kv_n = inp
        return dec[..., None] * state + kv_n, state

    s0 = jnp.zeros((B, GLA_HEADS, GLA_DK, GLA_DV), dtype=f32)
    _, s_prev = lax.scan(step, s0, (jnp.moveaxis(decay, 2, 0), jnp.moveaxis(kv, 2, 0)))
    s_prev = jnp.moveaxis(s_prev, 0, 2)
    o_inter = jnp.einsum('bhnid,bhndv->bhniv', q_e, s_prev)

    o = (o_intra + o_inter).transpose(0, 2, 3, 1, 4).reshape(B, S, GLA_HEADS, GLA_DV)
    o = rms_norm(o, gn_gain)
    o = o * jax.nn.silu(g_out.astype(f32).reshape(B, S, GLA_HEADS, GLA_DV))
    return o.reshape(B, S, GLA_V_W).astype(q.dtype)

def swa_sink_group(q, k, v, sinks, positions):
    B, S, _ = q.shape
    G = SWA_HEADS // SWA_KV_HEADS
    Wb = WINDOW
    NB = S // Wb
    hd = SWA_HEAD_DIM
    q = rope(q.reshape(B, S, SWA_HEADS, hd), positions)
    k = rope(k.reshape(B, S, SWA_KV_HEADS, hd), positions)
    v = v.reshape(B, S, SWA_KV_HEADS, hd)

    qb = q.reshape(B, NB, Wb, SWA_KV_HEADS, G, hd)
    kb = k.reshape(B, NB, Wb, SWA_KV_HEADS, hd)
    vb = v.reshape(B, NB, Wb, SWA_KV_HEADS, hd)
    pad = ((0, 0), (1, 0), (0, 0), (0, 0), (0, 0))
    kk = jnp.concatenate([jnp.pad(kb, pad)[:, :-1], kb], axis=2)
    vv = jnp.concatenate([jnp.pad(vb, pad)[:, :-1], vb], axis=2)

    s = jnp.einsum('bnqhgd,bnkhd->bnhgqk', qb, kk).astype(jnp.float32) * (hd ** -0.5)
    qi = jnp.arange(Wb)[:, None] + Wb
    ki = jnp.arange(2 * Wb)[None, :]
    band = (ki <= qi) & (qi - ki < WINDOW)
    has_prev = (jnp.arange(NB) > 0)[:, None, None] | (ki >= Wb)[None]
    mask = band[None] & has_prev
    s = jnp.where(mask[None, :, None, None, :, :], s, NEG_INF)

    sink_col = jnp.broadcast_to(
        sinks.astype(jnp.float32).reshape(1, 1, SWA_KV_HEADS, G, 1, 1),
        (B, NB, SWA_KV_HEADS, G, Wb, 1))
    p = jax.nn.softmax(jnp.concatenate([s, sink_col], axis=-1), axis=-1)[..., :-1]
    o = jnp.einsum('bnhgqk,bnkhd->bnqhgd', p.astype(vv.dtype), vv)
    return o.reshape(B, S, SWA_Q_W)

def conv_ffn(x, w_gate, w_up, conv_w, conv_b, w_down):
    S = x.shape[1]
    gte = x @ w_gate
    gp = jnp.pad(gte, ((0, 0), (CONV_WIDTH - 1, 0), (0, 0)))
    conv = conv_b
    for tap in range(CONV_WIDTH):
        conv = conv + conv_w[tap] * gp[:, tap:tap + S]
    h = jax.nn.silu(conv) * (x @ w_up)
    return h @ w_down

def setup_inputs(seed: int = 0) -> dict:
    key = jax.random.key(seed)
    ks = jax.random.split(key, 18)
    f32 = jnp.float32

    def nrm(k, shape, scale):
        return jax.random.normal(k, shape, dtype=f32) * scale

    x = jax.random.normal(ks[0], (BATCH, SEQ, D_MODEL), dtype=f32)
    offset = jax.random.randint(ks[1], (BATCH, 1), 0, 1024, dtype=jnp.int32)
    positions = offset + jnp.arange(SEQ, dtype=jnp.int32)[None, :]
    return {
        "x": x,
        "positions": positions,
        "attn_norm": 1.0 + nrm(ks[2], (DEPTH, D_MODEL), 0.02),
        "w_in": nrm(ks[3], (DEPTH, D_MODEL, IN_WIDTH), D_MODEL ** -0.5),
        "w_a_up": nrm(ks[4], (DEPTH, GLA_RANK, GLA_QK_W), GLA_RANK ** -0.5),
        "b_a_up": nrm(ks[5], (DEPTH, GLA_QK_W), 0.1),
        "gla_norm": 1.0 + nrm(ks[6], (DEPTH, GLA_DV), 0.02),
        "sinks": nrm(ks[7], (DEPTH, SWA_HEADS), 0.5),
        "w_out": nrm(ks[8], (DEPTH, MIX_WIDTH, D_MODEL), MIX_WIDTH ** -0.5),
        "ffn_norm": 1.0 + nrm(ks[9], (DEPTH, D_MODEL), 0.02),
        "w_gate": nrm(ks[10], (DEPTH, D_MODEL, D_FF), D_MODEL ** -0.5),
        "w_up": nrm(ks[11], (DEPTH, D_MODEL, D_FF), D_MODEL ** -0.5),
        "conv_w": nrm(ks[12], (DEPTH, CONV_WIDTH, D_FF), CONV_WIDTH ** -0.5),
        "conv_b": nrm(ks[13], (DEPTH, D_FF), 0.01),
        "w_down": nrm(ks[14], (DEPTH, D_FF, D_MODEL), D_FF ** -0.5),
        "final_norm": 1.0 + nrm(ks[15], (D_MODEL,), 0.02),
    }

def reference(x, positions, attn_norm, w_in, w_a_up, b_a_up, gla_norm, sinks, w_out,
              ffn_norm, w_gate, w_up, conv_w, conv_b, w_down, final_norm):
    h = x
    for l in range(DEPTH):
        u = rms_norm(h, attn_norm[l])
        gq, gk, gv, gg, ga, sq, sk, sv = split_cols(u @ w_in[l])
        o_gla = gla_group(gq, gk, gv, gg, ga, w_a_up[l], b_a_up[l], gla_norm[l])
        o_swa = swa_sink_group(sq, sk, sv, sinks[l], positions)
        h = h + jnp.concatenate([o_gla, o_swa.astype(h.dtype)], axis=-1) @ w_out[l]
        h = h + conv_ffn(rms_norm(h, ffn_norm[l]), w_gate[l], w_up[l], conv_w[l], conv_b[l], w_down[l])
    return rms_norm(h, final_norm)


_drawn_inputs = setup_inputs


def setup_inputs(seed=0):
    import zlib

    import numpy as np

    out = dict(_drawn_inputs(seed))
    spreads = {}
    factors = {'attn_norm': 3.042,
     'b_a_up': 2.957,
     'gla_norm': 6.344,
     'sinks': 64.0,
     'ffn_norm': 3.981,
     'conv_b': 30.061,
     'final_norm': 7.564}
    for name, (base, spread) in spreads.items():
        noise = np.random.default_rng([zlib.crc32(name.encode()), seed]).standard_normal(out[name].shape)
        drawn = base * np.exp(spread * noise) if base else spread * noise
        out[name] = __import__('jax').numpy.asarray(drawn.astype(out[name].dtype))
    for name, factor in factors.items():
        out[name] = (out[name] * factor).astype(out[name].dtype)
    return out
```

```python
from contextlib import ExitStack

import numpy as np
import concourse.bass as bass
from concourse import mybir

F32 = mybir.dt.float32
F32R = mybir.dt.float32r
I32 = mybir.dt.int32
U32 = mybir.dt.uint32
ALU = mybir.AluOpType
ACT = mybir.ActivationFunctionType
AX = mybir.AxisListType

P = 128
SEQ, DM = 512, 2048
TT = SEQ // P
KT = DM // P
NW = 512
QC = 4
GH, DK, DV, RANK, CH = 4, 128, 256, 16, 64
NCH = SEQ // CH
SH, KVH, HD, WIN = 16, 2, 64, 128
THETA, EPS, NEG = 10000.0, 1e-6, -1e30
DFF = 5632
FB = DFF // NW
FT = DFF // P
C_GQ, C_GK, C_GV, C_GG = 0, 512, 1024, 2048
C_GA = 3072
C_SQ = C_GA + RANK
C_SK = C_SQ + SH * HD
SMALL = RANK + 2 * KVH * HD

Q_KQ = 4
Q_REST = Q_KQ + 8
Q_OUT = 36
Q_FFN = Q_OUT + 16
Q_LOOP = Q_FFN + 8
Q_LAST = Q_LOOP + 12 * (FB - 1)
Q_END = Q_LAST + 4

S_PREP = 64
S_GLA = 72
S_KROPE = 84
S_QROPE = (97, 113)
S_SWA = 106
UNITS = KVH * TT * 4

R_ATTN, R_FFN, R_GN, R_BA, R_ALL = 0, 16, 32, 34, 38

TWO_PI = 6.283185307179586
TP1 = 6.28125
TP2 = float(np.float32(0.0019350051879882812))
TP3 = float(np.float32(TWO_PI - TP1 - TP2))
MAGIC = 12582912.0
PI_IN = 3.1415925


def unit_of(u):
    return u // 16, (u % 16) // 4, 4 * (u // 16) + u % 4


def loaded(q):
    return 16 * (q // 2 + 1) + (16 * min(q // 2 + 1, 2) if isinstance(q, int) else 0)


def build(nc, x, positions, attn_norm, w_in, w_a_up, b_a_up, gla_norm, sinks, w_out, ffn_norm,
          w_gate, w_up, conv_w, conv_b, w_down, final_norm, trig, out):
    ctx = ExitStack()
    top = [(nc.sbuf_base + 63) // 64 * 64]

    def place(name, shape, dt=F32, at=None):
        size = 4 * int(np.prod(shape[1:]))
        off = top[0] if at is None else at
        if at is None:
            top[0] += (size + 31) // 32 * 32
        return nc.alloc_sbuf_tensor_at(name, shape, dt, offset=off), off

    raw, _ = place("raw", [P, 2, QC * NW])
    whi, _ = place("whi", [P, 2, QC * NW], F32R)
    wlo, _ = place("wlo", [P, 2, QC * NW], F32R)
    ahi, _ = place("actT_hi", [P, KT, SEQ], F32R)
    alo, _ = place("actT_lo", [P, KT, SEQ], F32R)
    hres, o_w = place("hres", [P, TT, DM])
    kq, _ = place("kq", [P, 8, SEQ], at=o_w)
    v, _ = place("v", [P, TT, GH * DV], at=o_w + 4 * 8 * SEQ)
    sq, o_q = place("sq", [P, 8, SEQ])
    hT_hi, _ = place("hT_hi", [P, 4, SEQ], F32R, at=o_q)
    hT_lo, _ = place("hT_lo", [P, 4, SEQ], F32R, at=o_q + 4 * 4 * SEQ)
    ident, _ = place("ident", [P, P])
    swa_mask, _ = place("swa_mask", [P, 2 * WIN])
    gla_mask, _ = place("gla_mask", [P, P])
    cosT, _ = place("cosT", [P, SEQ])
    sinT, _ = place("sinT", [P, SEQ])
    keep, _ = place("keep", [P, SEQ])
    pc, _ = place("param_cols", [P, R_ALL])
    cw, _ = place("conv_cols", [P, 4, FT])
    sink_b, _ = place("sink_b", [P, SH])
    nsink, _ = place("nsink", [P, SH])
    trig_sb, _ = place("trig_sb", [P, 2])
    mhalf, _ = place("mhalf", [P, TT])
    ss, _ = place("ss", [P, TT, 4])
    ms, _ = place("ms", [P, TT])
    rstd, _ = place("rstd", [P, TT])
    kdup, _ = place("kdup", [P, KVH, SEQ])
    sv, _ = place("sv", [P, TT, KVH * HD])
    alow, _ = place("a_lowT", [RANK, SEQ])
    wau, _ = place("w_a_up_sb", [RANK, GH * DK])
    g_small, _ = place("gla_small", [P, 8 + 8 + 2 + 2 + 2])
    dec = g_small[:, 0:16].rearrange("p (a n) -> p a n", a=2)
    g_ss, g_ms, g_rs = g_small[:, 16:18], g_small[:, 18:20], g_small[:, 20:22]
    s_small, _ = place("swa_small", [P, 3, 5, 2])
    rtmp, o_rt = place("rtmp", [P, SEQ])
    bc, o_g = place("bc", [P, SEQ])
    t1, _ = place("t1", [P, SEQ])
    t2, _ = place("t2", [P, SEQ])
    t3, _ = place("t3", [P, SEQ])
    kdT, _ = place("kdT", [P, 2, TT, DK])
    S, _ = place("S", [P, 2, DV])
    sT, _ = place("sT", [P, 2, P])
    on, _ = place("on", [P, 2, DV])
    prob, o_p = place("prob", [P, 3, 2, 2 * WIN])
    pT, _ = place("pT", [P, 2, 4, P], at=o_g + 4 * SEQ)
    assert top[0] <= nc.sbuf_usable_end, (top[0], nc.sbuf_usable_end)
    diag, _ = place("diag", [P, TT, P], at=o_g)
    junk, _ = place("junk", [P, 2, SEQ], at=o_g + 20 * SEQ)
    prow, _ = place("prow", [P, 3, P], at=o_g + 2048)
    ang, _ = place("ang", [P, SEQ], at=o_g + 4096)
    turns, _ = place("turns", [P, SEQ], at=o_g + 6144)
    posb, _ = place("posb", [P, SEQ], I32, at=o_g + 8192)
    kraw, _ = place("kraw", [P, SEQ], at=o_p)
    gsil, _ = place("gsil", [P, 2, SEQ], at=o_g + 16 * SEQ)
    conv, _ = place("conv", [P, 2, SEQ], at=o_g + 4 * SEQ)
    sg, _ = place("sg", [P, 4, SEQ], at=o_g + 3 * 4 * SEQ)
    fgain, _ = place("fgain", [P, DM], at=o_g + 7 * 4 * SEQ)
    assert o_g + 11 * 4 * SEQ <= top[0]

    psA = ctx.enter_context(nc.psum_tensor("psA", [P, 4, 512], F32))
    psB = ctx.enter_context(nc.psum_tensor("psB", [P, 4, 512], F32))
    ps = (psA, psB)

    def sem(name):
        return ctx.enter_context(nc.semaphore(name))

    raw_loaded = [sem(f"raw_loaded{i}") for i in range(2)]
    hi_done, lo_done = sem("hi_done"), sem("lo_done")
    quad_used = sem("quad_used")
    x_loaded = [sem(f"x_loaded{t}") for t in range(TT)]
    x_back = [sem(f"x_back{t}") for t in range(TT)]
    rows_loaded, small_loaded = sem("rows_loaded"), sem("small_loaded")
    ident_ready, masks_ready = sem("ident_ready"), sem("masks_ready")
    pool_step, setup_step = sem("pool_step"), sem("setup_step")
    rows_turned, cols_ready = sem("rows_turned"), sem("cols_ready")
    sin_in, sin_out, trig_ready = sem("sin_in"), sem("sin_out"), sem("trig_ready")
    sq_sum, ms_step, ms_ready = sem("sq_sum"), sem("ms_step"), sem("ms_ready")
    rstd_ready, diag_ready = sem("rstd_ready"), sem("diag_ready")
    u_turned, u_hi, u_lo = sem("u_turned"), sem("u_hi"), sem("u_lo")
    proj_done, proj_free = sem("proj_done"), sem("proj_free")
    z_done, z_abs, z_exp, z_ln, z_min, z_la = (sem(n) for n in ("z_done", "z_abs", "z_exp", "z_ln", "z_min", "z_la"))
    bcum, e_pos, e_neg, to_last, e_last, e_dec = (sem(n) for n in ("bcum", "e_pos", "e_neg", "to_last", "e_last", "e_dec"))
    q_e, k_d, k_e, kd_turned, kd_ready = (sem(n) for n in ("q_e", "k_d", "k_e", "kd_turned", "kd_ready"))
    st_done, st_ready, gla_mm, kv_done, s_ready = (sem(n) for n in ("st_done", "st_ready", "gla_mm", "kv_done", "s_ready"))
    o_done, o_sq, o_ms, o_rstd, o_norm, o_turned, o_ready = (
        sem(n) for n in ("o_done", "o_sq", "o_ms", "o_rstd", "o_norm", "o_turned", "o_ready"))
    rope_step, k_ready, q_ready = sem("rope_step"), sem("k_ready"), sem("q_ready")
    sc_done, mx_done, negm, sinkm, p_exp, sink_exp = (sem(n) for n in ("sc_done", "mx_done", "negm", "sinkm", "p_exp", "sink_exp"))
    den, rden, p_ready, p_turned, pT_ready, pv_done, so_ready = (
        sem(n) for n in ("den", "rden", "p_ready", "p_turned", "pT_ready", "pv_done", "so_ready"))
    gate_silu, gla_mixed = sem("gate_silu"), sem("gla_mixed")
    mix_hi, mix_lo = sem("mix_hi"), sem("mix_lo")
    bank_done, bank_free = sem("bank_done"), sem("bank_free")
    conv_in, conv_mid, silu_done, h_hi, h_lo = (sem(n) for n in ("conv_in", "conv_mid", "silu_done", "h_hi", "h_lo"))
    gain_loaded, y_ready, stored = sem("gain_loaded"), sem("y_ready"), sem("stored")

    w_in_r = w_in.rearrange("o (c p) n -> p (o c) n", p=P)
    w_out_r = w_out.rearrange("o (c p) n -> p (o c) n", p=P)
    w_gate_r = w_gate.rearrange("o (c p) n -> p (o c) n", p=P)
    w_up_r = w_up.rearrange("o (c p) n -> p (o c) n", p=P)
    w_down_r = w_down.rearrange("o (c p) n -> p (o c) n", p=P)
    x_r = x.rearrange("o (t p) d -> p (o t) d", p=P)
    out_r = out.rearrange("o (t p) d -> p (o t) d", p=P)
    groups = [(C_GV, "v"), (C_GV + NW, "v"), (C_SQ, "sq"), (C_SQ + NW, "sq"), (C_GG, "gg"), (C_GG + NW, "gg")]

    def pf_after(G):
        return 3 + 4 * G

    def quad(t, slot, width=NW):
        return t[:, slot, 0:QC * width].rearrange("p (c n) -> p c n", c=QC)

    def proj_full(eng, G, f):
        if f < 3:
            eng.wait_ge(proj_done, 2 + 3 * (G - 1) + f + 1)
        else:
            eng.wait_ge(quad_used, 4 * G + 4)

    def bank_full(eng, g, f, q_last):
        if f < 3:
            eng.wait_ge(bank_done, 3 * g + f + 1)
        else:
            eng.wait_ge(quad_used, q_last + 1)

    block = ctx.enter_context(nc.Block())

    @block.sync
    def _(sp):
        def load(q, src, slot, first=False):
            sp.lower_ap_dma(src)
            if not first:
                sp.wait_ge(lo_done, q - 1)
            sp.dma_start(quad(raw, slot), src).then_inc(raw_loaded[slot], 16)

        for t in range(TT):
            sp.dma_start(hres[:, t, :], x_r[:, t, :]).then_inc(x_loaded[t], 16)
            if t == 0:
                sp.dma_start(prow[R_ATTN:R_ATTN + 16, 0, :], attn_norm.rearrange("o (r c) -> (o r) c", c=P)).then_inc(rows_loaded, 16)
                sp.dma_start(prow[R_FFN:R_FFN + 16, 0, :], ffn_norm.rearrange("o (r c) -> (o r) c", c=P)).then_inc(rows_loaded, 16)
                sp.dma_start(prow[R_GN:R_GN + 2, 0, :], gla_norm.rearrange("o (r c) -> (o r) c", c=P)).then_inc(rows_loaded, 16)
                sp.dma_start(prow[R_BA:R_BA + 4, 0, :], b_a_up.rearrange("o (r c) -> (o r) c", c=P)).then_inc(rows_loaded, 16)
                for tap in range(3):
                    sp.dma_start(prow[44 * (tap % 2):44 * (tap % 2) + 44, 1 + tap // 2, :],
                                 conv_w[0, tap, :].rearrange("(r c) -> r c", c=P)).then_inc(rows_loaded, 16)
                sp.dma_start(prow[44:88, 2, :], conv_b.rearrange("o (r c) -> (o r) c", c=P)).then_inc(rows_loaded, 16)
        for q in range(Q_KQ):
            if q >= 2:
                sp.wait_ge(lo_done, q - 1)
            dst = quad(raw, q % 2, SMALL)
            sp.dma_start(dst[:, :, 0:RANK], w_in_r[:, QC * q:QC * q + QC, C_GA:C_GA + RANK]).then_inc(raw_loaded[q % 2], 16)
            sp.dma_start(dst[:, :, RANK:SMALL], w_in_r[:, QC * q:QC * q + QC, C_SK:C_SK + SMALL - RANK]).then_inc(raw_loaded[q % 2], 16)
        with sp.Fori(0, 2) as i:
            for j in range(4):
                load(Q_KQ + 4 * i + j, w_in_r[:, QC * j:QC * j + QC, bass.ds(C_GK - NW * i, NW)], j % 2)
        for n, (col, _) in enumerate(groups):
            for j in range(4):
                load(Q_REST + 4 * n + j, w_in_r[:, QC * j:QC * j + QC, col:col + NW], j % 2)
        with sp.Fori(0, 4) as n:
            for j in range(4):
                kt = (8 + QC * j) % KT
                load(Q_OUT + 4 * n + j, w_out_r[:, kt:kt + QC, bass.ts(n, NW)], j % 2)
        for m, w in enumerate((w_gate_r, w_up_r)):
            for j in range(4):
                load(Q_FFN + 4 * m + j, w[:, QC * j:QC * j + QC, 0:NW], j % 2)
        with sp.Fori(1, FB) as b:
            q0 = Q_LOOP - 12 + 12 * b
            for j in range(4):
                load(q0 + j, w_gate_r[:, QC * j:QC * j + QC, bass.ts(b, NW)], j % 2)
            for n in range(4):
                load(q0 + 4 + n, w_down_r[:, bass.ds(QC * b - QC, QC), NW * n:NW * n + NW], n % 2)
            for j in range(4):
                load(q0 + 8 + j, w_up_r[:, QC * j:QC * j + QC, bass.ts(b, NW)], j % 2)
        for n in range(4):
            load(Q_LAST + n, w_down_r[:, QC * (FB - 1):QC * FB, NW * n:NW * n + NW], n % 2)
        for t in range(TT):
            sp.wait_ge(y_ready, t + 1)
            sp.dma_start(out_r[:, t, :], hres[:, t, :]).then_inc(stored, 16)
        sp.wait_ge(stored, 16 * TT)

    @block.gpsimd
    def _(pool):
        steps = [0]

        def step(ins):
            steps[0] += 1
            ins.then_inc(pool_step, 1)
            pool.wait_ge(pool_step, steps[0])

        pool.dma_start(trig_sb[:, :], trig).then_inc(small_loaded, 16)
        pool.dma_start(posb[:, :], positions.partition_broadcast(P).rearrange("p o s -> p (o s)")).then_inc(small_loaded, 16)
        pool.dma_start(sink_b[:, :], sinks.partition_broadcast(P).rearrange("p o s -> p (o s)")).then_inc(small_loaded, 16)
        pool.dma_start(wau[:, :], w_a_up.rearrange("o r n -> (o r) n")).then_inc(small_loaded, 16)
        step(pool.memset(ident[:, :], 0.0))
        pool.affine_select(out=ident[:, :], in_=ident[:, :], compare_op=ALU.not_equal, fill=1.0, base=0,
                           pattern=[[-1, P]], channel_multiplier=1).then_inc(ident_ready, 1)
        step(pool.memset(mhalf[:, :], -0.5))
        step(pool.memset(swa_mask[:, :], 0.0))
        step(pool.affine_select(out=swa_mask[:, :], in_=swa_mask[:, :], compare_op=ALU.is_gt, fill=NEG, base=0,
                                pattern=[[1, 2 * WIN]], channel_multiplier=-1))
        pool.affine_select(out=swa_mask[:, :], in_=swa_mask[:, :], compare_op=ALU.is_ge, fill=NEG, base=WIN,
                           pattern=[[-1, 2 * WIN]], channel_multiplier=1).then_inc(masks_ready, 1)
        step(pool.memset(gla_mask[:, :], 1.0))
        step(pool.affine_select(out=gla_mask[:, :], in_=gla_mask[:, :], compare_op=ALU.is_ge, fill=0.0, base=0,
                                pattern=[[1, P]], channel_multiplier=-1))
        pool.memset(gla_mask[0:CH, CH:P], 0.0).then_inc(masks_ready, 1)
        pool.memset(sT[:, :, :], 0.0).then_inc(masks_ready, 1)
        step(pool.memset(keep[:, :], 1.0))
        pool.memset(keep[:, :].rearrange("p (n c) -> p n c", c=CH)[:, :, 0:1], 0.0).then_inc(masks_ready, 1)

        def inverse_root(n, val, res):
            pool.wait_ge(ms_ready, n + 1)
            pool.tensor_tensor(res, val, mhalf[:, 0:1], ALU.pow).then_inc(rstd_ready, 1)

        for t in range(TT):
            inverse_root(t, ms[:, t:t + 1], rstd[:, t:t + 1])
        for n in range(GH * TT):
            pool.wait_ge(o_ms, n + 1)
            pool.tensor_tensor(g_rs[:, n % 2:n % 2 + 1], g_ms[:, n % 2:n % 2 + 1], mhalf[:, 0:1], ALU.pow).then_inc(o_rstd, 1)
        pool.wait_ge(mix_lo, KT)
        for t in range(TT):
            pool.dma_start(hres[:, t, :], x_r[:, t, :]).then_inc(x_back[t], 16)
        for t in range(TT):
            inverse_root(TT + t, ms[:, t:t + 1], rstd[:, t:t + 1])
        pool.dma_start(fgain[:, :], final_norm.partition_broadcast(P)).then_inc(gain_loaded, 16)
        for t in range(TT):
            inverse_root(2 * TT + t, ms[:, t:t + 1], rstd[:, t:t + 1])

    @block.scalar
    def _(act):
        def split_hi(q, slot, n=QC * NW, used=True):
            act.wait_ge(raw_loaded[slot], loaded(q) if isinstance(q, int) else 8 * (q - slot) + 48)
            if used:
                act.wait_ge(quad_used, q - 1)
            act.activation(whi[:, slot, 0:n], raw[:, slot, 0:n], ACT.Copy).then_inc(hi_done, 1)

        def square_sum(t, n, count, j):
            if not isinstance(count, int) or count >= 2:
                act.wait_ge(sq_sum, count - 1)
            act.activation(junk[:, j, :], hres[:, t, NW * n:NW * n + NW], ACT.Square,
                           accum_out=ss[:, t, n:n + 1]).then_inc(sq_sum, 1)

        def u_split_hi(r, ft):
            act.wait_ge(u_turned, KT * r + ft + 1)
            act.activation(ahi[:, ft, :], psB[:, ft % 4, :], ACT.Copy,
                           scale=pc[:, (R_ATTN, R_FFN)[r] + ft:(R_ATTN, R_FFN)[r] + ft + 1]).then_inc(u_hi, 1)

        act.wait_ge(small_loaded, 64)
        act.wait_ge(sin_in, 1)
        act.activation(sinT[:, :], ang[:, :], ACT.Sin, scale=trig_sb[:, 1:2]).then_inc(sin_out, 1)
        act.activation(cosT[:, :], ang[:, :], ACT.Sin, scale=0.5).then_inc(sin_out, 1)
        split_hi(0, 0, QC * SMALL, used=False)
        for t in range(TT):
            act.wait_ge(x_loaded[t], 16)
            for n in range(4):
                square_sum(t, n, 4 * t + n, n % 2)
        act.wait_ge(cols_ready, 2)
        for ft in range(KT):
            u_split_hi(0, ft)
            if ft == 1:
                split_hi(1, 1, QC * SMALL, used=False)
            if ft in (8, 12):
                split_hi(ft // 4, ft // 4 % 2, QC * SMALL)

        def gla_prep(h, k):
            if k == 0:
                act.wait_ge(z_done, h + 1)
                act.activation(t1[:, :], psB[:, 0, :], ACT.Abs, bias=pc[:, R_BA + h:R_BA + h + 1]).then_inc(z_abs, 1)
                act.wait_ge(z_abs, h + 1)
                act.activation(t1[:, :], t1[:, :], ACT.Exp, scale=-1.0).then_inc(z_exp, 1)
                act.wait_ge(z_exp, h + 1)
                act.activation(t1[:, :], t1[:, :], ACT.Ln, bias=1.0).then_inc(z_ln, 1)
            if k == 1:
                act.wait_ge(bcum, h + 1)
                act.activation(t1[:, :], bc[:, :], ACT.Exp, scale=1.0 / 16).then_inc(e_pos, 1)
                act.activation(t2[:, :], bc[:, :], ACT.Exp, scale=-1.0 / 16).then_inc(e_neg, 1)
                last = bc[:, :].rearrange("p (n c) -> p n c", c=CH)[:, :, CH - 1:CH].rearrange("p n c -> p (n c)")
                if h >= 2:
                    act.wait_ge(s_ready, 7 * (h - 1))
                act.activation(dec[:, h % 2, :], last, ACT.Exp, scale=1.0 / 16).then_inc(e_dec, 1)
                act.wait_ge(to_last, h + 1)
                act.activation(t3[:, :], t3[:, :], ACT.Exp, scale=1.0 / 16).then_inc(e_last, 1)
            if k == 4:
                act.wait_ge(kd_turned, h + 1)
                act.activation(kdT[:, h % 2, :, :], psB[:, 0, :].rearrange("p (t d) -> p t d", d=DK), ACT.Copy)\
                   .then_inc(kd_ready, 1)

        def gla_norm_out(m):
            src = psB[:, 2, 0:DV]
            act.wait_ge(o_done, m + 1)
            if m >= 2:
                act.wait_ge(o_turned, m - 1)
                act.wait_ge(o_ms, m - 1)
            act.activation(on[:, m % 2, :], src, ACT.Square, accum_out=g_ss[:, m % 2:m % 2 + 1]).then_inc(o_sq, 1)
            act.wait_ge(o_rstd, m + 1)
            act.activation(on[:, m % 2, :], src, ACT.Copy, scale=g_rs[:, m % 2:m % 2 + 1]).then_inc(o_norm, 1)

        def swa_exp(u):
            w = unit_of(u)[1] > 0
            c0 = 0 if w else WIN
            act.wait_ge(negm, u + 1)
            for e in range(2):
                act.activation(prob[:, u % 3, e, c0:], prob[:, u % 3, e, c0:], ACT.Exp,
                               bias=s_small[:, u % 3, 1, e:e + 1], scale=HD ** -0.5,
                               accum_out=s_small[:, u % 3, 3, e:e + 1]).then_inc(p_exp, 1)
            act.wait_ge(sinkm, u + 1)
            act.activation(s_small[:, u % 3, 2, :], s_small[:, u % 3, 2, :], ACT.Exp).then_inc(sink_exp, 1)

        def swa_pT(u):
            a = 0 if unit_of(u)[1] else 2
            act.wait_ge(p_turned, u + 1)
            if u >= 2:
                act.wait_ge(pv_done, u - 1)
            act.activation(pT[:, u % 2, a:, :], psB[:, 2, :].rearrange("p (a q) -> p a q", q=P)[:, a:, :], ACT.Copy)\
               .then_inc(pT_ready, 1)

        def swa_out(u):
            _, n, tile = unit_of(u)
            act.wait_ge(pv_done, u + 1)
            act.activation(sq[:, tile, P * n:P * n + P], psB[:, 3, 0:P], ACT.Copy)\
               .then_inc(so_ready, 1)

        def extras(s):
            for h in range(GH):
                if 0 <= s - (S_PREP + 8 * h) < 8:
                    gla_prep(h, s - (S_PREP + 8 * h))
            m = s - S_GLA
            if 0 <= m < 8 * GH and m % 2 == 1:
                gla_norm_out(m // 2)
            if 0 <= s - S_SWA < UNITS:
                swa_exp(s - S_SWA)
            if 0 <= s - S_SWA - 2 < UNITS:
                swa_pT(s - S_SWA - 2)
            if 0 <= s - S_SWA - 3 < UNITS:
                swa_out(s - S_SWA - 3)

        split_hi(4, 0)
        act.wait_ge(proj_done, 1)
        act.activation(kraw[:, :], psA[:, 0, :], ACT.Copy).then_inc(proj_free, 1)
        act.wait_ge(proj_done, 2)
        act.activation(sv[:, :, :], psA[:, 1, :].rearrange("p (t n) -> p t n", t=TT), ACT.Copy).then_inc(proj_free, 1)
        act.wait_ge(quad_used, Q_KQ)
        act.activation(alow[:, :], psA[0:RANK, 2, :], ACT.Copy).then_inc(proj_free, 1)
        with act.Fori(0, 2) as i:
            for j in range(4):
                split_hi(Q_KQ + 1 + 4 * i + j, (j + 1) % 2)
            for f in range(4):
                proj_full(act, i + 1, f)
                act.activation(kq[:, bass.ds(4 * i + f, 1), :].rearrange("p a s -> p (a s)"), psA[:, f, :], ACT.Copy).then_inc(proj_free, 1)
        for n, (_, kind) in enumerate(groups):
            for j in range(4):
                q = Q_REST + 4 * n + j
                if q + 1 < Q_OUT:
                    split_hi(q + 1, (j + 1) % 2)
                for s in range(4 * q, 4 * q + 4):
                    extras(s)
            if n < 5:
                for f in range(4):
                    proj_full(act, 3 + n, f)
                    if kind == "v":
                        act.activation(v[:, f, NW * n:NW * n + NW], psA[:, f, :], ACT.Copy).then_inc(proj_free, 1)
                    elif kind == "sq":
                        act.activation(sq[:, 4 * (n - 2) + f, :], psA[:, f, :], ACT.Copy).then_inc(proj_free, 1)
                    else:
                        if f >= 2:
                            act.wait_ge(gla_mixed, f - 1)
                        else:
                            act.wait_ge(o_ready, GH * TT)
                        act.activation(gsil[:, f % 2, :], psA[:, f, :], ACT.Silu).then_inc(proj_free, 1)

        split_hi(Q_OUT, 0)
        act.wait_ge(quad_used, Q_OUT)
        act.wait_ge(so_ready, UNITS)

        def mix_tile(m):
            kt = (8 + m) % KT
            if kt >= 8:
                act.activation(ahi[:, kt, :], sq[:, kt - 8, :], ACT.Copy).then_inc(mix_hi, 1)
            else:
                act.wait_ge(gla_mixed, kt + 1)
                act.activation(ahi[:, kt, :].rearrange("p (t c) -> p t c", t=TT), v[:, :, P * kt:P * kt + P], ACT.Copy)\
                   .then_inc(mix_hi, 1)

        mix_tile(0)
        mix_tile(1)
        for f in range(4):
            act.wait_ge(gla_mixed, 3 + f)
            act.activation(gsil[:, f % 2, :], psA[:, f, :], ACT.Silu).then_inc(proj_free, 1)
            mix_tile(2 + f)
        for m in range(6, KT):
            mix_tile(m)
        with act.Fori(0, 2) as i:
            for half in range(2):
                for j in range(4):
                    split_hi(Q_OUT + 1 + 8 * i + 4 * half + j, (j + 1) % 2)
                for t in range(TT):
                    act.wait_ge(bank_free, 8 * i + 4 * half + t + 1)
                    act.wait_ge(sq_sum, 16 + 8 * i + 4 * half + t - 1)
                    act.activation(junk[:, t % 2, :], hres[:, t, bass.ds(2 * NW * i + NW * half, NW)], ACT.Square,
                                   accum_out=ss[:, t, bass.ds(2 * i + half, 1)]).then_inc(sq_sum, 1)
        for ft in range(KT):
            u_split_hi(1, ft)
            if ft in (1, 9, 13):
                split_hi(Q_FFN + (1, 9, 13).index(ft) + 1, (1, 0, 1)[(1, 9, 13).index(ft)])

        def gate_in(b, j, g, q_last):
            bank_full(act, g, j, q_last)
            if not isinstance(b, int) or b or j >= 2:
                act.wait_ge(silu_done, 4 * b + j - 1)
            act.activation(conv[:, j % 2, :], psA[:, j, :], ACT.Identity, scale=cw[:, 2, bass.ds(4 * b + j, 1)],
                           bias=cw[:, 3, bass.ds(4 * b + j, 1)]).then_inc(conv_in, 1)

        def gate_silu_out(b, j, g):
            act.wait_ge(bank_free, 4 * g + j + 1)
            act.activation(sg[:, j, :], conv[:, j % 2, :], ACT.Silu).then_inc(silu_done, 1)

        def gate_evac(b, g, q_last, first=False):
            if not first:
                act.wait_ge(h_lo, 4 * b)
            gate_in(b, 0, g, q_last)
            for j in range(4):
                if j < 3:
                    gate_in(b, j + 1, g, q_last)
                gate_silu_out(b, j, g)

        def hidden_hi(b, g):
            for j in range(4):
                act.wait_ge(bank_free, 4 * g + j + 1)
                act.activation(hT_hi[:, j, :], sg[:, j, :], ACT.Copy).then_inc(h_hi, 1)

        split_hi(Q_FFN + 4, 0)
        split_hi(Q_FFN + 5, 1)
        gate_evac(0, 4, Q_FFN + 3, first=True)
        for j in range(2, 4):
            split_hi(Q_FFN + 4 + j, j % 2)
        split_hi(Q_LOOP, 0)
        with act.Fori(1, FB) as b:
            q0 = Q_LOOP - 12 + 12 * b
            g0 = 6 * b
            split_hi(q0 + 1, 1)
            hidden_hi(b - 1, g0 - 1)
            for j in range(1, 4):
                split_hi(q0 + j + 1, (j + 1) % 2)
            split_hi(q0 + 5, 1)
            gate_evac(b, g0, q0 + 3)
            for j in range(5, 12):
                split_hi(q0 + j + 1, (j + 1) % 2)
        hidden_hi(FB - 1, 6 * FB - 1)
        for n in range(4):
            if n < 3:
                split_hi(Q_LAST + n + 1, (n + 1) % 2)
            if n >= 1:
                for t in range(TT):
                    act.wait_ge(bank_free, 24 * FB + 4 * (n - 1) + t + 1)
                    square_sum(t, n - 1, 32 + 4 * (n - 1) + t, t % 2)
        for t in range(TT):
            act.wait_ge(bank_free, 24 * FB + 12 + t + 1)
            square_sum(t, 3, 32 + 12 + t, t % 2)

    @block.vector
    def _(dve):
        setups = [0]

        def step(ins):
            setups[0] += 1
            ins.then_inc(setup_step, 1)
            dve.wait_ge(setup_step, setups[0])

        def split_lo(q, slot, n=QC * NW):
            dve.wait_ge(hi_done, q + 1)
            dve.tensor_tensor(wlo[:, slot, 0:n], raw[:, slot, 0:n], whi[:, slot, 0:n].bitcast(F32), ALU.subtract)\
               .then_inc(lo_done, 1)

        def mean_square(r, t, count, with_diag=True):
            dve.wait_ge(sq_sum, count)
            dve.tensor_reduce(ms[:, t:t + 1], ss[:, t, :], AX.X, ALU.add).then_inc(ms_step, 1)
            dve.wait_ge(ms_step, TT * r + t + 1)
            dve.tensor_scalar(ms[:, t:t + 1], ms[:, t:t + 1], 1.0 / DM, EPS, ALU.mult, ALU.add).then_inc(ms_ready, 1)

        def make_diag(r, t):
            dve.wait_ge(rstd_ready, TT * r + t + 1)
            dve.tensor_scalar(diag[:, t, :], ident[:, :], rstd[:, t:t + 1], None, ALU.mult).then_inc(diag_ready, 1)

        def u_split_lo(r, ft):
            g = (R_ATTN, R_FFN)[r] + ft
            dve.wait_ge(u_hi, KT * r + ft + 1)
            dve.scalar_tensor_tensor(out=alo[:, ft, :], in0=psB[:, ft % 4, :], scalar=pc[:, g:g + 1],
                                     in1=ahi[:, ft, :].bitcast(F32), op0=ALU.mult, op1=ALU.subtract).then_inc(u_lo, 1)

        dve.wait_ge(small_loaded, 64)
        step(dve.tensor_scalar(ang[:, :], posb[:, :], trig_sb[:, 0:1], None, ALU.mult))
        step(dve.tensor_scalar(turns[:, :], ang[:, :], 1.0 / TWO_PI, MAGIC, ALU.mult, ALU.add))
        step(dve.tensor_scalar(turns[:, :], turns[:, :], -MAGIC, None, ALU.add))
        for part in (TP1, TP2, TP3):
            step(dve.scalar_tensor_tensor(out=ang[:, :], in0=turns[:, :], scalar=-part, in1=ang[:, :],
                                          op0=ALU.mult, op1=ALU.add))
        dve.tensor_scalar(ang[:, :], ang[:, :], PI_IN, -PI_IN, ALU.min, ALU.max).then_inc(sin_in, 1)
        dve.tensor_scalar(nsink[:, :], sink_b[:, :], -1.0, None, ALU.mult).then_inc(trig_ready, 1)
        dve.wait_ge(sin_out, 2)
        step(dve.scalar_tensor_tensor(out=cosT[:, :], in0=cosT[:, :], scalar=-2.0, in1=cosT[:, :],
                                      op0=ALU.mult, op1=ALU.mult))
        dve.tensor_scalar(cosT[:, :], cosT[:, :], 1.0, None, ALU.add).then_inc(trig_ready, 1)
        dve.wait_ge(rows_turned, 3)
        dve.tensor_copy(pc[:, :], psA[:, 0, 0:R_ALL]).then_inc(cols_ready, 1)
        dve.tensor_copy(cw[:, :, :], psA[:, 0, 64:64 + 4 * FT].rearrange("p (a f) -> p a f", a=4)).then_inc(cols_ready, 1)
        split_lo(0, 0, QC * SMALL)
        for t in range(TT):
            mean_square(0, t, 4 * t + 4)
        for t in range(TT):
            make_diag(0, t)
        dve.wait_ge(cols_ready, 2)
        for ft in range(KT):
            u_split_lo(0, ft)
            if ft == 1:
                split_lo(1, 1, QC * SMALL)
            if ft in (8, 12):
                split_lo(ft // 4, ft // 4 % 2, QC * SMALL)

        def gla_prep(h, k):
            kh, qh = kq[:, h, :], kq[:, 4 + h, :]
            if k == 0:
                dve.wait_ge(z_abs, h + 1)
                if h >= 1:
                    dve.wait_ge(e_neg, h)
                dve.tensor_scalar(t2[:, :], psB[:, 0, :], pc[:, R_BA + h:R_BA + h + 1], 0.0, ALU.add, ALU.min).then_inc(z_min, 1)
                dve.wait_ge(z_min, h + 1)
                dve.wait_ge(z_ln, h + 1)
                dve.tensor_tensor(t2[:, :], t2[:, :], t1[:, :], ALU.subtract).then_inc(z_la, 1)
                dve.wait_ge(z_la, h + 1)
                dve.tensor_tensor_scan(bc[:, :], keep[:, :], t2[:, :], 0.0, ALU.mult, ALU.add).then_inc(bcum, 1)
            if k == 1:
                dve.wait_ge(bcum, h + 1)
                if h >= 1:
                    dve.wait_ge(kd_turned, h)
                b3 = bc[:, :].rearrange("p (n c) -> p n c", c=CH)
                dve.tensor_tensor(t3[:, :].rearrange("p (n c) -> p n c", c=CH),
                                  b3[:, :, CH - 1:CH].broadcast_to([P, NCH, CH]), b3, ALU.subtract).then_inc(to_last, 1)
                dve.wait_ge(e_pos, h + 1)
                dve.scalar_tensor_tensor(out=qh, in0=qh, scalar=DK ** -0.5, in1=t1[:, :], op0=ALU.mult, op1=ALU.mult).then_inc(q_e, 1)
                dve.wait_ge(e_last, h + 1)
                dve.tensor_tensor(t3[:, :], t3[:, :], kh, ALU.mult).then_inc(k_d, 1)
                dve.wait_ge(e_neg, h + 1)
                dve.tensor_tensor(kh, kh, t2[:, :], ALU.mult).then_inc(k_e, 1)

        def gla_scores(m):
            dve.wait_ge(st_done, m + 1)
            if m >= 2:
                dve.wait_ge(gla_mm, m - 1)
            dve.copy_predicated(sT[:, m % 2, :], gla_mask[:, :].bitcast(U32), psB[:, 1, 0:P])\
               .then_inc(st_ready, 1)

        def gla_state(h, n):
            if n == 7:
                return
            kv = psB[:, 3, 0:DV]
            new = S[:, (n + 1) % 2, :]
            dve.wait_ge(kv_done, 7 * h + n + 1)
            if n == 0:
                if h >= 1:
                    dve.wait_ge(o_done, TT * h)
                dve.tensor_copy(new, kv).then_inc(s_ready, 1)
            else:
                dve.wait_ge(e_dec, h + 1)
                dve.wait_ge(s_ready, 7 * h + n)
                dve.scalar_tensor_tensor(out=new, in0=S[:, n % 2, :], scalar=dec[:, h % 2, n:n + 1], in1=kv,
                                         op0=ALU.mult, op1=ALU.add).then_inc(s_ready, 1)

        def gla_ms(m):
            dve.wait_ge(o_sq, m + 1)
            if m >= 2:
                dve.wait_ge(o_rstd, m - 1)
            dve.tensor_scalar(g_ms[:, m % 2:m % 2 + 1], g_ss[:, m % 2:m % 2 + 1], 1.0 / DV, EPS, ALU.mult, ALU.add).then_inc(o_ms, 1)

        def gla_out(m):
            h, c = m // TT, m % TT
            dve.wait_ge(o_turned, m + 1)
            for j in range(2):
                ins = dve.tensor_scalar(v[:, c, DV * h + P * j:DV * h + P * j + P], psB[:, 0, P * j:P * j + P],
                                        pc[:, R_GN + j:R_GN + j + 1], None, ALU.mult)
            ins.then_inc(o_ready, 1)

        rope_steps = [0]

        def rope(src, part):
            if part == 0:
                for a in range(0, P, 64):
                    dve.tensor_tensor(rtmp[a:a + 32, :], src[a + 32:a + 64, :], sinT[a + 32:a + 64, :], ALU.mult)
                    ins = dve.tensor_tensor(rtmp[a + 32:a + 64, :], src[a:a + 32, :], sinT[a:a + 32, :], ALU.mult)
                rope_steps[0] += 1
                ins.then_inc(rope_step, 1)
                dve.wait_ge(rope_step, rope_steps[0])
            else:
                rope_steps[0] += 1
                dve.tensor_tensor(src, src, cosT[:, :], ALU.mult).then_inc(rope_step, 1)
                dve.wait_ge(rope_step, rope_steps[0])
                return dve.tensor_tensor(src, src, rtmp[:, :], ALU.add)

        def swa_max(u):
            i, n, tile = unit_of(u)
            c0 = 0 if n else WIN
            k = s_small[:, u % 3, :, :]
            dve.wait_ge(sc_done, u + 1)
            if u >= 3:
                dve.wait_ge(p_turned, u - 2)
            for e in range(2):
                dve.tensor_tensor_reduce(out=prob[:, u % 3, e, c0:], in0=psB[:, e, c0:256],
                                         in1=swa_mask[:, c0:], scale=1.0, scalar=-3e38, op0=ALU.add, op1=ALU.max,
                                         accum_out=k[:, 0, e:e + 1]).then_inc(mx_done, 1)
            dve.wait_ge(mx_done, 2 * u + 2)
            hs = slice(2 * tile, 2 * tile + 2)
            dve.scalar_tensor_tensor(out=k[:, 1, :], in0=k[:, 0, :], scalar=-HD ** -0.5, in1=nsink[:, hs],
                                     op0=ALU.mult, op1=ALU.min).then_inc(negm, 1)
            dve.wait_ge(negm, u + 1)
            dve.tensor_tensor(k[:, 2, :], sink_b[:, hs], k[:, 1, :], ALU.add).then_inc(sinkm, 1)

        def swa_norm(u):
            c0 = 0 if unit_of(u)[1] else WIN
            k = s_small[:, u % 3, :, :]
            dve.wait_ge(p_exp, 2 * u + 2)
            dve.wait_ge(sink_exp, u + 1)
            dve.tensor_tensor(k[:, 3, :], k[:, 3, :], k[:, 2, :], ALU.add).then_inc(den, 1)
            dve.wait_ge(den, u + 1)
            dve.reciprocal(k[:, 4, :], k[:, 3, :]).then_inc(rden, 1)
            dve.wait_ge(rden, u + 1)
            for e in range(2):
                ins = dve.tensor_scalar(prob[:, u % 3, e, c0:], prob[:, u % 3, e, c0:], k[:, 4, e:e + 1], None, ALU.mult)
            ins.then_inc(p_ready, 1)

        def extras(s):
            for h in range(GH):
                if 0 <= s - (S_PREP + 8 * h) < 8:
                    gla_prep(h, s - (S_PREP + 8 * h))
            m = s - S_GLA
            if -1 <= m < 8 * GH - 1 and m % 2 == 1:
                gla_scores((m + 1) // 2)
            if 0 <= m < 8 * GH:
                gla_state(m // 8, m % 8)
                if m % 2 == 1:
                    gla_ms(m // 2)
            if 0 <= m - 2 < 8 * GH and m % 2 == 1:
                gla_out((m - 2) // 2)
            k = s - S_KROPE
            if k == 0:
                dve.wait_ge(proj_free, 1)
                dve.wait_ge(trig_ready, 2)
                rope(kraw[:, :], 0)
            if k == 1:
                ins = rope(kraw[:, :], 1)
                rope_steps[0] += 1
                ins.then_inc(rope_step, 1)
                dve.wait_ge(rope_step, rope_steps[0])
                for i in range(KVH):
                    for a in range(0, P, HD):
                        ins = dve.tensor_copy(kdup[a:a + HD, i, :], kraw[HD * i:HD * i + HD, :])
                ins.then_inc(k_ready, 1)
            for g in range(2):
                k = s - S_QROPE[g]
                if 0 <= k < 8:
                    f = 4 * g + k // 2
                    if k == 0:
                        dve.wait_ge(proj_free, pf_after(4 + g + 1))
                    if k % 2 == 0:
                        if f:
                            dve.wait_ge(q_ready, f)
                        rope(sq[:, f, :], 0)
                    else:
                        rope(sq[:, f, :], 1).then_inc(q_ready, 1)
            if 0 <= s - S_SWA < UNITS:
                swa_max(s - S_SWA)
                swa_norm(s - S_SWA)

        split_lo(4, 0)
        with dve.Fori(0, 2) as i:
            for j in range(4):
                split_lo(Q_KQ + 1 + 4 * i + j, (j + 1) % 2)
        def mix_gate(f):
            dve.wait_ge(proj_free, pf_after(6) + f + 1)
            tile = v[:, :, P * f:P * f + P]
            dve.tensor_tensor(tile, tile, gsil[:, f % 2, :].rearrange("p (t c) -> p t c", t=TT), ALU.mult).then_inc(gla_mixed, 1)

        for n, (_, kind) in enumerate(groups):
            for j in range(4):
                q = Q_REST + 4 * n + j
                if n == 5 and j == 0:
                    for f in range(4):
                        mix_gate(f)
                if q + 1 < Q_OUT:
                    split_lo(q + 1, (j + 1) % 2)
                for s in range(4 * q, 4 * q + 4):
                    extras(s)

        split_lo(Q_OUT, 0)

        def mix_tile(m):
            kt = (8 + m) % KT
            dve.wait_ge(mix_hi, m + 1)
            if kt >= 8:
                dve.tensor_tensor(alo[:, kt, :], sq[:, kt - 8, :], ahi[:, kt, :].bitcast(F32), ALU.subtract).then_inc(mix_lo, 1)
            else:
                dve.tensor_tensor(alo[:, kt, :].rearrange("p (t c) -> p t c", t=TT), v[:, :, P * kt:P * kt + P],
                                  ahi[:, kt, :].bitcast(F32).rearrange("p (t c) -> p t c", t=TT), ALU.subtract).then_inc(mix_lo, 1)

        mix_tile(0)
        mix_tile(1)
        for f in range(4):
            mix_gate(4 + f)
            mix_tile(2 + f)
        for m in range(6, KT):
            mix_tile(m)

        def add_h(t, col, g, q_last, b):
            bank_full(dve, g, t, q_last)
            dve.tensor_tensor(hres[:, t, col], hres[:, t, col], ps[b][:, t, :], ALU.add).then_inc(bank_free, 1)

        with dve.Fori(0, 2) as i:
            for half in range(2):
                for j in range(4):
                    split_lo(Q_OUT + 1 + 8 * i + 4 * half + j, (j + 1) % 2)
                for t in range(TT):
                    dve.wait_ge(x_back[t], 16)
                    add_h(t, bass.ds(2 * NW * i + NW * half, NW), 2 * i + half, Q_OUT + 8 * i + 4 * half + 3, half)
        for t in range(TT):
            mean_square(1, t, 16 + 12 + t + 1)
        for t in range(TT):
            make_diag(1, t)
        for ft in range(KT):
            u_split_lo(1, ft)
            if ft in (1, 9, 13):
                split_lo(Q_FFN + (1, 9, 13).index(ft) + 1, (1, 0, 1)[(1, 9, 13).index(ft)])

        def gate_evac(b, g, q_last):
            for j in range(4):
                tap = bass.ds(4 * b + j, 1)
                dve.wait_ge(conv_in, 4 * b + j + 1)
                dve.scalar_tensor_tensor(out=conv[:, j % 2, 1:], in0=psA[:, j, 0:SEQ - 1], scalar=cw[:, 1, tap],
                                         in1=conv[:, j % 2, 1:], op0=ALU.mult, op1=ALU.add).then_inc(conv_mid, 1)
                dve.wait_ge(conv_mid, 4 * b + j + 1)
                dve.scalar_tensor_tensor(out=conv[:, j % 2, 2:], in0=psA[:, j, 0:SEQ - 2], scalar=cw[:, 0, tap],
                                         in1=conv[:, j % 2, 2:], op0=ALU.mult, op1=ALU.add).then_inc(bank_free, 1)

        def up_evac(b, g, q_last):
            def low(j):
                dve.wait_ge(h_hi, 4 * b + j + 1)
                dve.tensor_tensor(hT_lo[:, j, :], sg[:, j, :], hT_hi[:, j, :].bitcast(F32), ALU.subtract).then_inc(h_lo, 1)
            for j in range(4):
                bank_full(dve, g, j, q_last)
                dve.wait_ge(silu_done, 4 * b + j + 1)
                dve.tensor_tensor(sg[:, j, :], sg[:, j, :], psB[:, j, :], ALU.mult).then_inc(bank_free, 1)
                if j >= 1:
                    low(j - 1)
            low(3)

        def down_evac(n, g, q_last, b):
            for t in range(TT):
                add_h(t, slice(NW * n, NW * n + NW), g, q_last, b)

        split_lo(Q_FFN + 4, 0)
        split_lo(Q_FFN + 5, 1)
        gate_evac(0, 4, Q_FFN + 3)
        for j in range(2, 4):
            split_lo(Q_FFN + 4 + j, j % 2)
        split_lo(Q_LOOP, 0)
        with dve.Fori(1, FB) as b:
            q0 = Q_LOOP - 12 + 12 * b
            g0 = 6 * b
            split_lo(q0 + 1, 1)
            up_evac(b - 1, g0 - 1, q0 - 1)
            for j in range(1, 4):
                split_lo(q0 + j + 1, (j + 1) % 2)
            split_lo(q0 + 5, 1)
            gate_evac(b, g0, q0 + 3)
            for n in range(4):
                split_lo(q0 + 6 + n, n % 2)
                down_evac(n, g0 + 1 + n, q0 + 4 + n, 1 - n % 2)
            for j in range(9, 12):
                split_lo(q0 + j + 1, (j + 1) % 2)
        up_evac(FB - 1, 6 * FB - 1, Q_LAST - 1)
        for n in range(4):
            if n < 3:
                split_lo(Q_LAST + n + 1, (n + 1) % 2)
            down_evac(n, 6 * FB + n, Q_LAST + n, n % 2)
        for t in range(TT):
            mean_square(2, t, 32 + 12 + t + 1)
        dve.wait_ge(gain_loaded, 16)
        for t in range(TT):
            dve.wait_ge(rstd_ready, 2 * TT + t + 1)
            dve.scalar_tensor_tensor(out=hres[:, t, :], in0=hres[:, t, :], scalar=rstd[:, t:t + 1], in1=fgain[:, :],
                                     op0=ALU.mult, op1=ALU.mult).then_inc(y_ready, 1)

    @block.tensor
    def _(pe):
        def three(dst, a, b, first, last):
            pe.matmul(dst, a[0], b[0], start=first, stop=False, skip_group_check=True)
            pe.matmul(dst, a[0], b[1], start=False, stop=False, skip_group_check=True)
            return pe.matmul(dst, a[1], b[0], start=False, stop=last, skip_group_check=True)

        def weights(slot, c, a, n, width=NW):
            return tuple(quad(w, slot, width)[:, c, a:a + n] for w in (whi, wlo))

        def acts(k, a=0, n=SEQ):
            return ahi[:, k, a:a + n], alo[:, k, a:a + n]

        def feature_major(bank, slot, c, k, first, last):
            for f in range(4):
                yield f, lambda f=f: three(bank[:, f, :], weights(slot, c, P * f, P), acts(k), first, last)

        def token_major(bank, slot, c, lhs, first, last):
            for t in range(TT):
                yield t, lambda t=t: three(bank[:, t, :], lhs(t), weights(slot, c, 0, NW), first, last)

        def turn_u(r, ft):
            if ft == 0:
                pe.wait_ge(diag_ready, TT * r + TT)
            if ft >= 4:
                pe.wait_ge(u_lo, KT * r + ft - 3)
            for t in range(TT):
                ins = pe.matmul(psB[:, ft % 4, P * t:P * t + P], hres[:, t, P * ft:P * ft + P], diag[:, t, :],
                                start=True, stop=True)
            ins.then_inc(u_turned, 1)

        pe.wait_ge(ident_ready, 1)
        pe.wait_ge(rows_loaded, 16 * 8)
        pe.transpose(psA[:, 0, 0:R_ALL], prow[0:R_ALL, 0, :], ident[0:R_ALL, 0:R_ALL]).then_inc(rows_turned, 1)
        for m in range(2):
            pe.transpose(psA[:, 0, 64 + 88 * m:64 + 88 * m + 88], prow[0:88, 1 + m, :], ident[0:88, 0:88]).then_inc(rows_turned, 1)

        for ft in range(4):
            turn_u(0, ft)
        pe.wait_ge(cols_ready, 2)
        for k in range(KT):
            q, c = k // QC, k % QC
            if c == 0:
                pe.wait_ge(lo_done, q + 1)
            pe.wait_ge(u_lo, k + 1)
            first, last = k == 0, k == KT - 1
            ins = three(psA[:, 0, :], weights(q % 2, c, RANK, P, SMALL), acts(k), first, last)
            if last:
                ins.then_inc(proj_done, 1)
            for t in range(TT):
                ins = three(psA[:, 1, P * t:P * t + P], acts(k, P * t, P), weights(q % 2, c, RANK + P, P, SMALL),
                            first and t == 0, last)
            if last:
                ins.then_inc(proj_done, 1)
            ins = three(psA[:, 2, :], weights(q % 2, c, 0, P, SMALL), acts(k), first, last)
            if c == QC - 1:
                ins.then_inc(quad_used, 1)
            if k + 4 < KT:
                turn_u(0, k + 4)

        def group(q0, bank, kind, done, free=None, extras=None, ready=None, kts=range(KT)):
            for j in range(4):
                pe.wait_ge(lo_done, q0 + j + 1)
                for c in range(QC):
                    n = QC * j + c
                    k, first, last = kts[n], n == 0, n == KT - 1
                    if ready:
                        ready(n)
                    for f in range(4):
                        if first and free:
                            free(f)
                        if kind == "token":
                            ins = three(bank[:, f, :], acts(k, P * f, P), weights(j % 2, c, 0, NW), first, last)
                        else:
                            ins = three(bank[:, f, :], weights(j % 2, c, P * f, P), acts(k), first, last)
                        if last and f < 3:
                            ins.then_inc(done, 1)
                    if c == QC - 1:
                        ins.then_inc(quad_used, 1)
                    if extras:
                        extras(4 * (q0 + j) + c)

        def turns_before(s):
            return max(0, (s - (S_GLA + 3) + 1) // 2)

        def gla_prep(h, k, s):
            if k == 0:
                if h == 0:
                    pe.wait_ge(u_lo, KT)
                    pe.wait_ge(proj_free, 3)
                else:
                    pe.wait_ge(kd_ready, h)
                    if turns_before(s):
                        pe.wait_ge(o_ready, turns_before(s))
                pe.matmul(psB[:, 0, :], wau[:, DK * h:DK * h + DK], alow[:, :], start=True, stop=True).then_inc(z_done, 1)
            if k == 4:
                pe.wait_ge(k_d, h + 1)
                if turns_before(s):
                    pe.wait_ge(o_ready, turns_before(s))
                for t in range(TT):
                    ins = pe.transpose(psB[:, 0, DK * t:DK * t + DK], t3[:, P * t:P * t + P], ident[:, :])
                ins.then_inc(kd_turned, 1)

        def gla_scores(m):
            h, c = m // TT, m % TT
            pe.wait_ge(k_e, h + 1)
            pe.wait_ge(q_e, h + 1)
            if m == 0:
                pe.wait_ge(masks_ready, 4)
            if m >= 1:
                pe.wait_ge(st_ready, m)
            pe.matmul(psB[:, 1, 0:P], kq[:, h, P * c:P * c + P], kq[:, 4 + h, P * c:P * c + P],
                      start=True, stop=True).then_inc(st_done, 1)

        def gla_step(h, n):
            c, b, m = n // 2, n % 2, TT * h + n // 2
            vt = v[:, c, DV * h:DV * h + DV]
            o = psB[:, 2, 0:DV]
            if b == 0:
                pe.wait_ge(st_ready, m + 1)
                if m >= 1:
                    pe.wait_ge(o_norm, m)
                ins = pe.matmul(o, sT[:, m % 2, :], vt, start=True, stop=False, skip_group_check=True)
            if n >= 1:
                pe.wait_ge(s_ready, 7 * h + n)
                ins = pe.matmul(o[CH * b:CH * b + CH, :], kq[:, 4 + h, CH * n:CH * n + CH], S[:, n % 2, :],
                                start=False, stop=True, skip_group_check=True)
            if b == 0:
                ins.then_inc(gla_mm, 1)
            else:
                ins.then_inc(o_done, 1)
            if n < 7:
                pe.wait_ge(kd_ready, h + 1)
                if h + n:
                    pe.wait_ge(s_ready, 7 * h + n)
                rows = slice(CH * b, CH * b + CH)
                pe.matmul(psB[:, 3, 0:DV], kdT[rows, h % 2, c, :], v[rows, c, DV * h:DV * h + DV],
                          start=True, stop=True).then_inc(kv_done, 1)

        def gla_turn(m, s):
            pe.wait_ge(o_norm, m + 1)
            pe.wait_ge(z_min, min(GH, (s - S_PREP) // 8 + 1))
            pe.wait_ge(kd_ready, min(GH, (s - S_PREP - 4) // 8 + 1))
            if m >= 1:
                pe.wait_ge(o_ready, m)
            for j in range(2):
                ins = pe.transpose(psB[:, 0, P * j:P * j + P], on[:, m % 2, P * j:P * j + P], ident[:, :])
            ins.then_inc(o_turned, 1)

        def swa_scores(u):
            i, n, tile = unit_of(u)
            a = P * (n - 1) if n else 0
            c0 = 0 if n else WIN
            pe.wait_ge(k_ready, 1)
            pe.wait_ge(q_ready, tile + 1)
            if u == 0:
                pe.wait_ge(kd_ready, GH)
                pe.wait_ge(o_ready, GH * TT)
            if u >= 1:
                pe.wait_ge(mx_done, 2 * u)
            for e in range(2):
                rows = slice(HD * e, HD * e + HD)
                ins = pe.matmul(psB[:, e, c0:256], sq[rows, tile, P * n:P * n + P],
                                kdup[rows, i, a:P * n + P], start=True, stop=True)
            ins.then_inc(sc_done, 1)

        def swa_turn(u):
            a = 0 if unit_of(u)[1] else 1
            pe.wait_ge(p_ready, u + 1)
            if u >= 1:
                pe.wait_ge(pT_ready, u)
            for kt in range(a, 2):
                for e in range(2):
                    ins = pe.transpose(psB[:, 2, P * (2 * kt + e):P * (2 * kt + e) + P], prob[:, u % 3, e, P * kt:P * kt + P],
                                       ident[:, :])
            ins.then_inc(p_turned, 1)

        def swa_pv(u):
            i, n, _ = unit_of(u)
            a = 0 if n else 1
            pe.wait_ge(pT_ready, u + 1)
            if u >= 1:
                pe.wait_ge(so_ready, u)
            for e in range(2):
                for kt in range(a, 2):
                    ins = pe.matmul(psB[HD * e:HD * e + HD, 3, 0:P],
                                    sv[:, n - 1 + kt, HD * i:HD * i + HD], pT[:, u % 2, 2 * kt + e, :],
                                    start=(kt == a), stop=(kt == 1))
            ins.then_inc(pv_done, 1)

        def extras(s):
            for h in range(GH):
                if 0 <= s - (S_PREP + 8 * h) < 8:
                    gla_prep(h, s - (S_PREP + 8 * h), s)
            m = s - S_GLA
            if 0 <= m < 8 * GH:
                gla_step(m // 8, m % 8)
            if -1 <= m < 8 * GH - 1 and m % 2 == 1:
                gla_scores((m + 1) // 2)
            if 0 <= m - 2 < 8 * GH and m % 2 == 1:
                gla_turn((m - 2) // 2, s)
            u = s - S_SWA
            if 0 <= u < UNITS:
                swa_scores(u)
            if 0 <= u - 2 < UNITS:
                swa_turn(u - 2)
            if 0 <= u - 3 < UNITS:
                swa_pv(u - 3)

        with pe.Fori(0, 2) as i:
            group(Q_KQ + 4 * i, psA, "feature", proj_done, free=lambda f: pe.wait_ge(proj_free, 4 * i + min(f + 1, 3)))
        for n, (_, kind) in enumerate(groups):
            group(Q_REST + 4 * n, psA, "token" if kind == "v" else "feature", proj_done,
                  free=lambda f: pe.wait_ge(proj_free, pf_after(1 + n) + f + 1), extras=extras)

        pe.wait_ge(proj_free, pf_after(7) + 4)
        with pe.Fori(0, 2) as i:
            for half in range(2):
                group(Q_OUT + 8 * i + 4 * half, ps[half], "token", bank_done,
                      ready=(lambda n: pe.wait_ge(mix_lo, n + 1)) if half == 0 else None,
                      kts=[(8 + n) % KT for n in range(KT)])
        for ft in range(4):
            turn_u(1, ft)

        def down(n, q, bank, b, g, free=True):
            pe.wait_ge(lo_done, q + 1)
            for c in range(QC):
                pe.wait_ge(h_lo, 4 * b + c + 1)
                for t in range(TT):
                    if c == 0:
                        pe.wait_ge(bank_free, 4 * (g - 2) + t + 1)
                    ins = three(bank[:, t, :], (hT_hi[:, c, P * t:P * t + P], hT_lo[:, c, P * t:P * t + P]),
                                weights(n % 2, c, 0, NW), c == 0, c == QC - 1)
                    if c == QC - 1 and t < 3:
                        ins.then_inc(bank_done, 1)
            ins.then_inc(quad_used, 1)

        def freed(g):
            return lambda f: pe.wait_ge(bank_free, 4 * (g - 2) + f + 1)

        group(Q_FFN, psA, "feature", bank_done, free=freed(4), ready=lambda n: pe.wait_ge(u_lo, KT + n + 1),
              extras=lambda s: turn_u(1, s - 4 * Q_FFN + 4) if s - 4 * Q_FFN + 4 < KT else None)
        group(Q_FFN + 4, psB, "feature", bank_done, free=freed(5))
        with pe.Fori(1, FB) as b:
            q0 = Q_LOOP - 12 + 12 * b
            g0 = 6 * b
            group(q0, psA, "feature", bank_done, free=freed(g0))
            for n in range(4):
                down(n, q0 + 4 + n, ps[1 - n % 2], b - 1, g0 + 1 + n)
            group(q0 + 8, psB, "feature", bank_done, free=freed(g0 + 5))
        for n in range(4):
            down(n, Q_LAST + n, ps[n % 2], FB - 1, 6 * FB + n)

    ctx.close()


_INS = ["x", "positions", "attn_norm", "w_in", "w_a_up", "b_a_up", "gla_norm", "sinks", "w_out", "ffn_norm",
        "w_gate", "w_up", "conv_w", "conv_b", "w_down", "final_norm"]


def kernel(**inputs):
    import numpy as _np
    import concourse.bacc as _bacc
    from concourse import mybir as _mybir
    from concourse.bass_utils import run_bass_kernel_spmd as _run

    nc = _bacc.Bacc("TRN2", target_bir_lowering=False, num_devices=1)
    arrays, args = {}, []
    for name in _INS:
        a = _np.ascontiguousarray(inputs[name])
        arrays[f"in_{name}"] = a
        args.append(nc.dram_tensor(f"in_{name}", a.shape, _mybir.dt.from_np(a.dtype), kind="ExternalInput").ap())
    half = HD // 2
    part = _np.arange(P)
    freq = (THETA ** (-(part % half).astype(_np.float32) / _np.float32(half))).astype(_np.float32)
    sign = _np.where(part % HD < half, 1.0, -1.0).astype(_np.float32)
    arrays["trig"] = _np.ascontiguousarray(_np.stack([freq, sign], axis=1))
    args.append(nc.dram_tensor("trig", (P, 2), _mybir.dt.float32, kind="ExternalInput").ap())
    args.append(nc.dram_tensor("out", (1, SEQ, DM), _mybir.dt.float32, kind="ExternalOutput").ap())
    build(nc, *args)
    r = _run(nc, [arrays], core_ids=[0])
    return r.results[0]["out"]
```

```python
from contextlib import ExitStack

import numpy as np
import concourse.bass as bass
from concourse import mybir

F32 = mybir.dt.float32
F32R = mybir.dt.float32r
I32 = mybir.dt.int32
U32 = mybir.dt.uint32
ALU = mybir.AluOpType
ACT = mybir.ActivationFunctionType
AX = mybir.AxisListType

P = 128
SEQ, DM = 512, 2048
TT = SEQ // P
KT = DM // P
NW = 512
QC = 4
GH, DK, DV, RANK, CH = 4, 128, 256, 16, 64
NCH = SEQ // CH
SH, KVH, HD, WIN = 16, 2, 64, 128
THETA, EPS, NEG = 10000.0, 1e-6, -1e30
DFF = 5632
FB = DFF // NW
FT = DFF // P
C_GQ, C_GK, C_GV, C_GG = 0, 512, 1024, 2048
C_GA = 3072
C_SQ = C_GA + RANK
C_SK = C_SQ + SH * HD
SMALL = RANK + 2 * KVH * HD

Q_KQ = 4
Q_REST = Q_KQ + 8
Q_OUT = 36
Q_FFN = Q_OUT + 16
Q_LOOP = Q_FFN + 8
Q_LAST = Q_LOOP + 12 * (FB - 1)
Q_END = Q_LAST + 4
LAST = ((0, 2), (1, 2), (0, 3), (1, 3), (2, 2), (2, 3), (3, 2), (3, 3))

S_PREP = 64
S_GLA = 72
S_KROPE = 84
S_QROPE = (97, 113)
S_SWA = 106
UNITS = KVH * TT * 4

R_ATTN, R_FFN, R_GN, R_BA, R_ALL = 0, 16, 32, 34, 38

TWO_PI = 6.283185307179586
TP1 = 6.28125
TP2 = float(np.float32(0.0019350051879882812))
TP3 = float(np.float32(TWO_PI - TP1 - TP2))
MAGIC = 12582912.0
PI_IN = 3.1415925
Y_ACT = 768


def unit_of(u):
    return u // 16, (u % 16) // 4, 4 * (u // 16) + u % 4


def loaded(q):
    return 16 * (q // 2 + 1) + 32 * min(q // 2 + 1, 2)


def build(nc, x, positions, attn_norm, w_in, w_a_up, b_a_up, gla_norm, sinks, w_out, ffn_norm,
          w_gate, w_up, conv_w, conv_b, w_down, final_norm, trig, out):
    ctx = ExitStack()
    top = [(nc.sbuf_base + 63) // 64 * 64]

    def place(name, shape, dt=F32, at=None):
        size = 4 * int(np.prod(shape[1:]))
        off = top[0] if at is None else at
        if at is None:
            top[0] += (size + 31) // 32 * 32
        return nc.alloc_sbuf_tensor_at(name, shape, dt, offset=off), off

    raw, _ = place("raw", [P, 2, QC * NW])
    whi, _ = place("whi", [P, 2, QC * NW], F32R)
    wlo, _ = place("wlo", [P, 2, QC * NW], F32R)
    ahi, _ = place("actT_hi", [P, KT, SEQ], F32R)
    alo, _ = place("actT_lo", [P, KT, SEQ], F32R)
    hres, o_w = place("hres", [P, TT, DM])
    kq, _ = place("kq", [P, 8, SEQ], at=o_w)
    v, _ = place("v", [P, TT, GH * DV], at=o_w + 4 * 8 * SEQ)
    kk_hi, _ = place("swa_k_hi", [P, KVH, SEQ], F32R, at=o_w)
    kk_lo, _ = place("swa_k_lo", [P, KVH, SEQ], F32R, at=o_w + 4 * KVH * SEQ)
    qs, _ = place("swa_q_split", [P, 3, 2, P], F32R, at=o_w + 8 * KVH * SEQ)
    sq, o_q = place("sq", [P, 8, SEQ])
    hT_hi, _ = place("hT_hi", [P, 4, SEQ], F32R, at=o_q)
    hT_lo, _ = place("hT_lo", [P, 4, SEQ], F32R, at=o_q + 4 * 4 * SEQ)
    ident, _ = place("ident", [P, P])
    swa_mask, _ = place("swa_mask", [P, 2 * WIN])
    gla_mask, _ = place("gla_mask", [P, P])
    cosT, _ = place("cosT", [P, SEQ])
    sinT, _ = place("sinT", [P, SEQ])
    keep, _ = place("keep", [P, SEQ])
    pc, _ = place("param_cols", [P, R_ALL])
    cw, _ = place("conv_cols", [P, 4, FT])
    sink_b, _ = place("sink_b", [P, SH])
    nsink, _ = place("nsink", [P, SH])
    trig_sb, _ = place("trig_sb", [P, 2])
    mhalf, _ = place("mhalf", [P, TT])
    ones, _ = place("ones", [P, P])
    rB, _ = place("rstd_bcast", [P, SEQ])
    ss, _ = place("ss", [P, TT, 4])
    ms, _ = place("ms", [P, TT])
    rstd, _ = place("rstd", [P, TT])
    kdup, _ = place("kdup", [P, KVH, SEQ])
    sv, _ = place("sv", [P, TT, KVH * HD])
    alow, _ = place("a_lowT", [RANK, SEQ])
    atok, _ = place("a_low", [P, TT, RANK])
    wau, _ = place("w_a_up_sb", [RANK, GH * DK])
    g_small, _ = place("gla_small", [P, 8 + 8 + 2 + 2 + 2])
    dec = g_small[:, 0:16].rearrange("p (a n) -> p a n", a=2)
    g_ss, g_ms, g_rs = g_small[:, 16:18], g_small[:, 18:20], g_small[:, 20:22]
    s_small, _ = place("swa_small", [P, 3, 5, 2])
    rtmp, o_rt = place("rtmp", [P, SEQ])
    bc, o_g = place("bc", [P, SEQ])
    t1, _ = place("t1", [P, SEQ])
    t2, _ = place("t2", [P, SEQ])
    t3, _ = place("t3", [P, SEQ])
    kdT, _ = place("kdT", [P, 2, TT, DK])
    S, _ = place("S", [P, 2, DV])
    sT, _ = place("sT", [P, 2, P])
    on, _ = place("on", [P, 2, DV])
    prob, o_p = place("prob", [P, 3, 2, 2 * WIN])
    pT, _ = place("pT", [P, 2, 4, P], at=o_g + 4 * SEQ)
    assert top[0] <= nc.sbuf_usable_end, (top[0], nc.sbuf_usable_end)
    diag, _ = place("diag", [P, TT, P], at=o_g)
    junk, _ = place("junk", [P, 2, SEQ], at=o_g + 20 * SEQ)
    prow, _ = place("prow", [P, 3, P], at=o_g + 2048)
    ang, _ = place("ang", [P, SEQ], at=o_g + 4096)
    turns, _ = place("turns", [P, SEQ], at=o_g + 6144)
    posb, _ = place("posb", [P, SEQ], I32, at=o_g + 8192)
    kraw, _ = place("kraw", [P, SEQ], at=o_p)
    gsil, _ = place("gsil", [P, 4, SEQ], at=o_g + 16 * SEQ)
    conv, _ = place("conv", [P, 2, SEQ], at=o_g + 4 * SEQ)
    gate, _ = place("gate", [P, 2, SEQ], at=o_rt)
    sg, _ = place("sg", [P, 4, SEQ], at=o_g + 3 * 4 * SEQ)
    fgain, _ = place("fgain", [P, DM], at=o_g + 7 * 4 * SEQ)
    assert o_g + 11 * 4 * SEQ <= top[0]

    psA = ctx.enter_context(nc.psum_tensor("psA", [P, 4, 512], F32))
    psB = ctx.enter_context(nc.psum_tensor("psB", [P, 4, 512], F32))
    ps = (psA, psB)

    def sem(name):
        return ctx.enter_context(nc.semaphore(name))

    raw_loaded = [sem(f"raw_loaded{i}") for i in range(2)]
    hi_done, lo_done = sem("hi_done"), sem("lo_done")
    quad_used = sem("quad_used")
    x_loaded = [sem(f"x_loaded{n}") for n in range(4)]
    x_back = [sem(f"x_back{t}") for t in range(TT)]
    rows_loaded, small_loaded = sem("rows_loaded"), sem("small_loaded")
    ident_ready, masks_ready = sem("ident_ready"), sem("masks_ready")
    pool_step, setup_step = sem("pool_step"), sem("setup_step")
    rows_turned, cols_ready = sem("rows_turned"), sem("cols_ready")
    sin_in, sin_out, trig_ready = sem("sin_in"), sem("sin_out"), sem("trig_ready")
    sq_sum, ms_step, ms_ready = sem("sq_sum"), sem("ms_step"), sem("ms_ready")
    rstd_ready, diag_ready = sem("rstd_ready"), sem("diag_ready")
    a_ready, a_turned, alow_ready = sem("a_ready"), sem("a_turned"), sem("alow_ready")
    rb_done, rb_ready = sem("rb_done"), sem("rb_ready")
    last_done = sem("last_done")
    silu_scaled, conv_done = sem("silu_scaled"), sem("conv_done")
    g_scaled, hg_ready, y_act = sem("g_scaled"), sem("hg_ready"), sem("y_act")
    u_turned, u_hi, u_lo = sem("u_turned"), sem("u_hi"), sem("u_lo")
    proj_done, proj_free = sem("proj_done"), sem("proj_free")
    z_done, z_abs, z_exp, z_ln, z_min, z_la = (sem(n) for n in ("z_done", "z_abs", "z_exp", "z_ln", "z_min", "z_la"))
    bcum, e_pos, e_neg, to_last, e_last, e_dec = (sem(n) for n in ("bcum", "e_pos", "e_neg", "to_last", "e_last", "e_dec"))
    q_e, k_d, k_e, kd_turned, kd_ready = (sem(n) for n in ("q_e", "k_d", "k_e", "kd_turned", "kd_ready"))
    st_done, st_ready, gla_mm, kv_done, s_ready = (sem(n) for n in ("st_done", "st_ready", "gla_mm", "kv_done", "s_ready"))
    o_done, o_sq, o_ms, o_rstd, o_norm, o_turned, o_ready = (
        sem(n) for n in ("o_done", "o_sq", "o_ms", "o_rstd", "o_norm", "o_turned", "o_ready"))
    rope_step, k_ready, q_ready = sem("rope_step"), sem("k_ready"), sem("q_ready")
    k_hi, k_lo, q_hi, q_lo = sem("k_hi"), sem("k_lo"), sem("q_hi"), sem("q_lo")
    sc_done, mx_done, negm, sinkm, p_exp, sink_exp = (sem(n) for n in ("sc_done", "mx_done", "negm", "sinkm", "p_exp", "sink_exp"))
    den, rden, p_ready, p_turned, pT_ready, pv_done, so_ready = (
        sem(n) for n in ("den", "rden", "p_ready", "p_turned", "pT_ready", "pv_done", "so_ready"))
    gate_silu, gla_mixed = sem("gate_silu"), sem("gla_mixed")
    mix_hi, mix_lo = sem("mix_hi"), sem("mix_lo")
    bank_done, bank_free = sem("bank_done"), sem("bank_free")
    conv_in, conv_mid, silu_done, h_hi, h_lo = (sem(n) for n in ("conv_in", "conv_mid", "silu_done", "h_hi", "h_lo"))
    gain_loaded, y_ready, stored = sem("gain_loaded"), sem("y_ready"), sem("stored")

    w_in_r = w_in.rearrange("o (c p) n -> p (o c) n", p=P)
    w_out_r = w_out.rearrange("o (c p) n -> p (o c) n", p=P)
    w_gate_r = w_gate.rearrange("o (c p) n -> p (o c) n", p=P)
    w_up_r = w_up.rearrange("o (c p) n -> p (o c) n", p=P)
    w_down_r = w_down.rearrange("o (c p) n -> p (o c) n", p=P)
    x_r = x.rearrange("o (t p) d -> p (o t) d", p=P)
    out_r = out.rearrange("o (t p) d -> p (o t) d", p=P)
    groups = [(C_GV, "v"), (C_GV + NW, "v"), (C_SQ, "sq"), (C_SQ + NW, "sq"), (C_GG, "gg"), (C_GG + NW, "gg")]

    def pf_after(G):
        return 3 + 4 * G

    def quad(t, slot, width=NW):
        return t[:, slot, 0:QC * width].rearrange("p (c n) -> p c n", c=QC)

    def proj_full(eng, G, f):
        if f < 3:
            before = 0 if isinstance(G, int) and G == 0 else 3 * G - 1
            eng.wait_ge(proj_done, before + f + 1)
        else:
            eng.wait_ge(quad_used, 4 * G + 4)

    def bank_full(eng, g, f, q_last):
        if f < 3:
            eng.wait_ge(bank_done, 3 * g + f + 1)
        else:
            eng.wait_ge(quad_used, q_last + 1)

    block = ctx.enter_context(nc.Block())

    @block.sync
    def _(sp):
        def load(q, src, slot, first=False):
            sp.lower_ap_dma(src)
            if not first:
                sp.wait_ge(lo_done, q - 1)
            sp.dma_start(quad(raw, slot), src).then_inc(raw_loaded[slot], 16)

        def load_narrow(q):
            if q >= 2:
                sp.wait_ge(lo_done, q - 1)
            dst = quad(raw, q % 2, SMALL)
            rows = w_in_r[:, QC * q:QC * q + QC, :]
            for to, col, n in ((0, C_SK, P), (P, C_GA, RANK), (P + RANK, C_SK + P, P)):
                sp.dma_start(dst[:, :, to:to + n], rows[:, :, col:col + n]).then_inc(raw_loaded[q % 2], 16)

        for n in range(4):
            sp.dma_start(hres[:, :, NW * n:NW * n + NW], x_r[:, :, NW * n:NW * n + NW]).then_inc(x_loaded[n], 16)
            if n == 0:
                sp.dma_start(prow[R_ATTN:R_ATTN + 16, 0, :], attn_norm.rearrange("o (r c) -> (o r) c", c=P)).then_inc(rows_loaded, 16)
                sp.dma_start(prow[R_FFN:R_FFN + 16, 0, :], ffn_norm.rearrange("o (r c) -> (o r) c", c=P)).then_inc(rows_loaded, 16)
                sp.dma_start(prow[R_GN:R_GN + 2, 0, :], gla_norm.rearrange("o (r c) -> (o r) c", c=P)).then_inc(rows_loaded, 16)
                sp.dma_start(prow[R_BA:R_BA + 4, 0, :], b_a_up.rearrange("o (r c) -> (o r) c", c=P)).then_inc(rows_loaded, 16)
                for tap in range(3):
                    sp.dma_start(prow[44 * (tap % 2):44 * (tap % 2) + 44, 1 + tap // 2, :],
                                 conv_w[0, tap, :].rearrange("(r c) -> r c", c=P)).then_inc(rows_loaded, 16)
                sp.dma_start(prow[44:88, 2, :], conv_b.rearrange("o (r c) -> (o r) c", c=P)).then_inc(rows_loaded, 16)
            if n < 2:
                load_narrow(n)
        for q in range(2, Q_KQ):
            load_narrow(q)
        with sp.Fori(0, 2) as i:
            for j in range(4):
                load(Q_KQ + 4 * i + j, w_in_r[:, QC * j:QC * j + QC, bass.ds(C_GK - NW * i, NW)], j % 2)
        for n, (col, _) in enumerate(groups):
            for j in range(4):
                load(Q_REST + 4 * n + j, w_in_r[:, QC * j:QC * j + QC, col:col + NW], j % 2)
        with sp.Fori(0, 4) as n:
            for j in range(4):
                kt = (8 + QC * j) % KT
                load(Q_OUT + 4 * n + j, w_out_r[:, kt:kt + QC, bass.ts(n, NW)], j % 2)
        for m, w in enumerate((w_gate_r, w_up_r)):
            for j in range(4):
                load(Q_FFN + 4 * m + j, w[:, QC * j:QC * j + QC, 0:NW], j % 2)
        with sp.Fori(1, FB) as b:
            q0 = Q_LOOP - 12 + 12 * b
            for j in range(4):
                load(q0 + j, w_gate_r[:, QC * j:QC * j + QC, bass.ts(b, NW)], j % 2)
            for n in range(4):
                load(q0 + 4 + n, w_down_r[:, bass.ds(QC * b - QC, QC), NW * n:NW * n + NW], n % 2)
            for j in range(4):
                load(q0 + 8 + j, w_up_r[:, QC * j:QC * j + QC, bass.ts(b, NW)], j % 2)
        for n in range(4):
            load(Q_LAST + n, w_down_r[:, QC * (FB - 1):QC * FB, NW * n:NW * n + NW], n % 2)
        for t in range(TT):
            sp.wait_ge(y_ready, 2 * t + 2)
            sp.wait_ge(y_act, t + 1)
            sp.dma_start(out_r[:, t, :], hres[:, t, :]).then_inc(stored, 16)
        sp.wait_ge(stored, 16 * TT)

    @block.gpsimd
    def _(pool):
        steps = [0]

        def step(ins):
            steps[0] += 1
            ins.then_inc(pool_step, 1)
            pool.wait_ge(pool_step, steps[0])

        step(pool.memset(ident[:, :], 0.0))
        pool.affine_select(out=ident[:, :], in_=ident[:, :], compare_op=ALU.not_equal, fill=1.0, base=0,
                           pattern=[[-1, P]], channel_multiplier=1).then_inc(ident_ready, 1)
        pool.memset(ones[:, :], 1.0).then_inc(ident_ready, 1)
        pool.dma_start(trig_sb[:, :], trig).then_inc(small_loaded, 16)
        pool.dma_start(posb[:, :], positions.partition_broadcast(P).rearrange("p o s -> p (o s)")).then_inc(small_loaded, 16)
        pool.dma_start(sink_b[:, :], sinks.partition_broadcast(P).rearrange("p o s -> p (o s)")).then_inc(small_loaded, 16)
        pool.dma_start(wau[:, :], w_a_up.rearrange("o r n -> (o r) n")).then_inc(small_loaded, 16)
        step(pool.memset(mhalf[:, :], -0.5))
        step(pool.memset(swa_mask[:, :], 0.0))
        step(pool.affine_select(out=swa_mask[:, :], in_=swa_mask[:, :], compare_op=ALU.is_gt, fill=NEG, base=0,
                                pattern=[[1, 2 * WIN]], channel_multiplier=-1))
        pool.affine_select(out=swa_mask[:, :], in_=swa_mask[:, :], compare_op=ALU.is_ge, fill=NEG, base=WIN,
                           pattern=[[-1, 2 * WIN]], channel_multiplier=1).then_inc(masks_ready, 1)
        step(pool.memset(gla_mask[:, :], 1.0))
        step(pool.affine_select(out=gla_mask[:, :], in_=gla_mask[:, :], compare_op=ALU.is_ge, fill=0.0, base=0,
                                pattern=[[1, P]], channel_multiplier=-1))
        pool.memset(gla_mask[0:CH, CH:P], 0.0).then_inc(masks_ready, 1)
        pool.memset(sT[:, :, :], 0.0).then_inc(masks_ready, 1)
        step(pool.memset(keep[:, :], 1.0))
        pool.memset(keep[:, :].rearrange("p (n c) -> p n c", c=CH)[:, :, 0:1], 0.0).then_inc(masks_ready, 1)

        def inverse_root(n, val, res):
            pool.wait_ge(ms_ready, n + 1)
            pool.tensor_tensor(res, val, mhalf[:, 0:1], ALU.pow).then_inc(rstd_ready, 1)

        for t in range(TT):
            inverse_root(t, ms[:, t:t + 1], rstd[:, t:t + 1])

        def swa_q_lo(u):
            _, n, tile = unit_of(u)
            pool.wait_ge(q_hi, u + 1)
            for e in range(2):
                rows, other = slice(HD * e, HD * e + HD), slice(HD * (1 - e), HD * (1 - e) + HD)
                ins = pool.tensor_tensor(qs[other, u % 3, e, :], sq[rows, tile, P * n:P * n + P],
                                        qs[rows, u % 3, e, :].bitcast(F32), ALU.subtract)
            ins.then_inc(q_lo, 1)

        for n in range(GH * TT):
            pool.wait_ge(o_ms, n + 1)
            pool.tensor_tensor(g_rs[:, n % 2:n % 2 + 1], g_ms[:, n % 2:n % 2 + 1], mhalf[:, 0:1], ALU.pow).then_inc(o_rstd, 1)
        for u in range(UNITS):
            swa_q_lo(u)
        pool.wait_ge(mix_lo, KT)
        for t in range(TT):
            pool.dma_start(hres[:, t, :], x_r[:, t, :]).then_inc(x_back[t], 16)
        for t in range(TT):
            inverse_root(TT + t, ms[:, t:t + 1], rstd[:, t:t + 1])
        pool.dma_start(fgain[:, :], final_norm.partition_broadcast(P)).then_inc(gain_loaded, 16)

        def scale_silu(b):
            for j in range(4):
                pool.wait_ge(silu_done, 4 * b + j + 1)
                pool.tensor_tensor(sg[:, j, :], sg[:, j, :], rB[:, :], ALU.mult).then_inc(silu_scaled, 1)

        pool.wait_ge(rb_ready, 2)
        scale_silu(0)
        with pool.Fori(1, FB) as b:
            scale_silu(b)
        pool.wait_ge(gain_loaded, 16)

        def gain(t, n, count):
            pool.wait_ge(sq_sum, count)
            col = slice(NW * n, NW * n + NW)
            pool.tensor_tensor(hres[:, t, col], hres[:, t, col], fgain[:, col], ALU.mult).then_inc(hg_ready, 1)

        for n in range(2):
            for t in range(TT):
                gain(t, n, 32 + TT * n + t + 1)
        for k, (t, n) in enumerate(LAST):
            if n == 2:
                gain(t, n, 40 + k + 1)
            else:
                inverse_root(2 * TT + t, ms[:, t:t + 1], rstd[:, t:t + 1])

    @block.scalar
    def _(act):
        def split_hi(q, slot, n=QC * NW, used=True):
            act.wait_ge(raw_loaded[slot], loaded(q) if isinstance(q, int) else 8 * (q - slot) + 80)
            if used:
                act.wait_ge(quad_used, q - 1)
            act.activation(whi[:, slot, 0:n], raw[:, slot, 0:n], ACT.Copy).then_inc(hi_done, 1)

        def square_sum(t, n, count, j):
            if not isinstance(count, int) or count >= 2:
                act.wait_ge(sq_sum, count - 1)
            act.activation(junk[:, j, :], hres[:, t, NW * n:NW * n + NW], ACT.Square,
                           accum_out=ss[:, t, n:n + 1]).then_inc(sq_sum, 1)

        def u_split_hi(r, ft):
            act.wait_ge(u_turned, KT * r + ft + 1)
            act.activation(ahi[:, (ft, (8 + ft) % KT)[r], :], psB[:, ft % 4, :], ACT.Copy,
                           scale=pc[:, (R_ATTN, R_FFN)[r] + ft:(R_ATTN, R_FFN)[r] + ft + 1]).then_inc(u_hi, 1)

        act.wait_ge(cols_ready, 2)
        for ft in range(KT):
            u_split_hi(0, ft)
            if ft == 0:
                split_hi(0, 0, QC * SMALL, used=False)
            if ft % 4 == 0:
                act.wait_ge(x_loaded[ft // 4], 16)
            square_sum(ft % 4, ft // 4, ft, ft % 2)
            if ft == 3:
                split_hi(1, 1, QC * SMALL, used=False)
            if ft in (8, 12):
                split_hi(ft // 4, ft // 4 % 2, QC * SMALL)
        def gla_prep(h, k):
            if k == 0:
                act.wait_ge(z_done, h + 1)
                act.activation(t1[:, :], psB[:, 0, :], ACT.Abs, bias=pc[:, R_BA + h:R_BA + h + 1]).then_inc(z_abs, 1)
                act.wait_ge(z_abs, h + 1)
                act.activation(t1[:, :], t1[:, :], ACT.Exp, scale=-1.0).then_inc(z_exp, 1)
                act.wait_ge(z_exp, h + 1)
                act.activation(t1[:, :], t1[:, :], ACT.Ln, bias=1.0).then_inc(z_ln, 1)
            if k == 2:
                act.wait_ge(bcum, h + 1)
                act.activation(t1[:, :], bc[:, :], ACT.Exp, scale=1.0 / 16).then_inc(e_pos, 1)
                act.activation(t2[:, :], bc[:, :], ACT.Exp, scale=-1.0 / 16).then_inc(e_neg, 1)
                last = bc[:, :].rearrange("p (n c) -> p n c", c=CH)[:, :, CH - 1:CH].rearrange("p n c -> p (n c)")
                if h >= 2:
                    act.wait_ge(s_ready, 7 * (h - 1))
                act.activation(dec[:, h % 2, :], last, ACT.Exp, scale=1.0 / 16).then_inc(e_dec, 1)
            if k == 3:
                act.wait_ge(to_last, h + 1)
                act.activation(t3[:, :], t3[:, :], ACT.Exp, scale=1.0 / 16).then_inc(e_last, 1)
            if k == 4:
                act.wait_ge(kd_turned, h + 1)
                act.activation(kdT[:, h % 2, :, :], psB[:, 0, :].rearrange("p (t d) -> p t d", d=DK), ACT.Copy)\
                   .then_inc(kd_ready, 1)

        def gla_square(m):
            act.wait_ge(o_done, m + 1)
            if m >= 2:
                act.wait_ge(o_turned, m - 1)
                act.wait_ge(o_ms, m - 1)
            act.activation(on[:, m % 2, :], psB[:, 2, 0:DV], ACT.Square, accum_out=g_ss[:, m % 2:m % 2 + 1]).then_inc(o_sq, 1)

        def gla_norm_out(m):
            act.wait_ge(o_rstd, m + 1)
            act.activation(on[:, m % 2, :], psB[:, 2, 0:DV], ACT.Copy, scale=g_rs[:, m % 2:m % 2 + 1]).then_inc(o_norm, 1)

        def swa_k_hi():
            act.wait_ge(k_ready, 1)
            act.wait_ge(o_done, GH * TT)
            act.activation(kk_hi[:, :, :], kdup[:, :, :], ACT.Copy).then_inc(k_hi, 1)

        def swa_q_hi(u):
            _, n, tile = unit_of(u)
            act.wait_ge(q_ready, tile + 1)
            if u >= 3:
                act.wait_ge(sc_done, u - 2)
            for e in range(2):
                rows = slice(HD * e, HD * e + HD)
                ins = act.activation(qs[rows, u % 3, e, :], sq[rows, tile, P * n:P * n + P], ACT.Copy)
            ins.then_inc(q_hi, 1)

        def swa_exp(u):
            w = unit_of(u)[1] > 0
            c0 = 0 if w else WIN
            act.wait_ge(negm, u + 1)
            for e in range(2):
                act.activation(prob[:, u % 3, e, c0:], prob[:, u % 3, e, c0:], ACT.Exp,
                               bias=s_small[:, u % 3, 1, e:e + 1], scale=HD ** -0.5,
                               accum_out=s_small[:, u % 3, 3, e:e + 1]).then_inc(p_exp, 1)
            act.wait_ge(sinkm, u + 1)
            act.activation(s_small[:, u % 3, 2, :], s_small[:, u % 3, 2, :], ACT.Exp).then_inc(sink_exp, 1)

        def swa_pT(u):
            a = 0 if unit_of(u)[1] else 2
            act.wait_ge(p_turned, u + 1)
            if u >= 2:
                act.wait_ge(pv_done, u - 1)
            act.activation(pT[:, u % 2, a:, :], psB[:, 2, :].rearrange("p (a q) -> p a q", q=P)[:, a:, :], ACT.Copy)\
               .then_inc(pT_ready, 1)

        def swa_out(u):
            _, n, tile = unit_of(u)
            act.wait_ge(pv_done, u + 1)
            act.activation(sq[:, tile, P * n:P * n + P], psB[:, 3, 0:P], ACT.Copy)\
               .then_inc(so_ready, 1)

        def extras(s):
            m = s - S_GLA
            if 0 <= m < 8 * GH and m % 2 == 1:
                gla_square(m // 2)
                gla_norm_out(m // 2)
            for h in range(GH):
                if 0 <= s - (S_PREP + 8 * h) < 8:
                    gla_prep(h, s - (S_PREP + 8 * h))
            if s == S_SWA - 2:
                swa_k_hi()
                swa_q_hi(0)
                swa_q_hi(1)
            if 2 <= s - S_SWA + 2 < UNITS:
                swa_q_hi(s - S_SWA + 2)
            if 0 <= s - S_SWA - 2 < UNITS:
                swa_pT(s - S_SWA - 2)
            if 0 <= s - S_SWA < UNITS:
                swa_exp(s - S_SWA)
            if 0 <= s - S_SWA - 3 < UNITS:
                swa_out(s - S_SWA - 3)

        def gate_silu_part(g):
            for f in range(4 * g, 4 * g + 4):
                act.wait_ge(g_scaled, f + 1)
                act.activation(gsil[:, f % 4, :], gsil[:, f % 4, :], ACT.Silu).then_inc(gate_silu, 1)

        split_hi(4, 0)
        split_hi(5, 1)
        act.wait_ge(small_loaded, 64)
        act.wait_ge(sin_in, 1)
        act.activation(sinT[:, :], ang[:, :], ACT.Sin, scale=trig_sb[:, 1:2]).then_inc(sin_out, 1)
        act.activation(cosT[:, :], ang[:, :], ACT.Sin, scale=0.5).then_inc(sin_out, 1)
        with act.Fori(0, 2) as i:
            for j in range(1, 5):
                split_hi(Q_KQ + 1 + 4 * i + j, (j + 1) % 2)
        for n, (_, kind) in enumerate(groups):
            for j in range(4):
                q = Q_REST + 4 * n + j
                if Q_REST < q < Q_OUT - 1:
                    split_hi(q + 1, (j + 1) % 2)
                for s in range(4 * q, 4 * q + 4):
                    if s == 4 * Q_REST + 16 * n + 15 and kind == "v":
                        for f in range(4):
                            proj_full(act, 3 + n, f)
                            act.activation(v[:, f, NW * n:NW * n + NW], psA[:, f, :], ACT.Copy, scale=rstd[:, f:f + 1])\
                               .then_inc(proj_free, 1)
                    extras(s)

        split_hi(Q_OUT, 0)
        gate_silu_part(0)
        act.wait_ge(quad_used, Q_OUT)
        act.wait_ge(so_ready, UNITS)

        def mix_tile(m):
            kt = (8 + m) % KT
            if kt >= 8:
                act.activation(ahi[:, kt, :], sq[:, kt - 8, :], ACT.Copy).then_inc(mix_hi, 1)
            else:
                act.wait_ge(gla_mixed, kt + 1)
                act.activation(ahi[:, kt, :].rearrange("p (t c) -> p t c", t=TT), v[:, :, P * kt:P * kt + P], ACT.Copy)\
                   .then_inc(mix_hi, 1)

        for m in range(KT):
            if m == 4:
                gate_silu_part(1)
            mix_tile(m)
            if m % 4 == 3:
                split_hi(Q_OUT + m // 4 + 1, (m // 4 + 1) % 2)
        def h_square(n, t):
            act.wait_ge(bank_free, 4 * n + t + 1)
            act.wait_ge(sq_sum, 16 + 4 * n + t - 1)
            act.activation(junk[:, t % 2, :], hres[:, t, bass.ts(n, NW)], ACT.Square,
                           accum_out=ss[:, t, bass.ds(n, 1)]).then_inc(sq_sum, 1)

        for t in range(TT):
            h_square(0, t)
        with act.Fori(1, 3) as n:
            for j in range(4):
                split_hi(Q_OUT + 1 + 4 * n + j, (j + 1) % 2)
            for t in range(TT):
                h_square(n, t)
        for ft in range(12):
            u_split_hi(1, ft)
            if ft % 3 == 1:
                split_hi(Q_OUT + 13 + ft // 3, (1 + ft // 3) % 2)
        split_hi(Q_FFN + 1, 1)
        for ft in range(12, KT):
            u_split_hi(1, ft)
        for t in range(TT):
            square_sum(t, 3, 28 + t, t % 2)
        for j in range(2, 4):
            split_hi(Q_FFN + j, j % 2)

        def gate_in(b, j, g):
            act.wait_ge(bank_free, 4 * g + j + 1)
            if not isinstance(b, int) or b or j >= 2:
                act.wait_ge(silu_done, 4 * b + j - 1)
            act.activation(conv[:, j % 2, :], gate[:, j % 2, :], ACT.Identity, scale=cw[:, 2, bass.ds(4 * b + j, 1)],
                           bias=cw[:, 3, bass.ds(4 * b + j, 1)]).then_inc(conv_in, 1)

        def gate_silu_out(b, j):
            act.wait_ge(conv_done, 4 * b + j + 1)
            act.activation(sg[:, j, :], conv[:, j % 2, :], ACT.Silu).then_inc(silu_done, 1)

        def gate_evac(b, g, first=False):
            if not first:
                act.wait_ge(h_lo, 4 * b)
            gate_in(b, 0, g)
            for j in range(4):
                if j < 3:
                    gate_in(b, j + 1, g)
                gate_silu_out(b, j)

        def hidden_hi(b, g):
            for j in range(4):
                act.wait_ge(bank_free, 4 * g + j + 1)
                act.activation(hT_hi[:, j, :], sg[:, j, :], ACT.Copy).then_inc(h_hi, 1)

        split_hi(Q_FFN + 4, 0)
        split_hi(Q_FFN + 5, 1)
        gate_evac(0, 4, first=True)
        for j in range(2, 4):
            split_hi(Q_FFN + 4 + j, j % 2)
        split_hi(Q_LOOP, 0)
        with act.Fori(1, FB) as b:
            q0 = Q_LOOP - 12 + 12 * b
            g0 = 6 * b
            split_hi(q0 + 1, 1)
            hidden_hi(b - 1, g0 - 1)
            for j in range(1, 4):
                split_hi(q0 + j + 1, (j + 1) % 2)
            split_hi(q0 + 5, 1)
            gate_evac(b, g0)
            for j in range(5, 12):
                split_hi(q0 + j + 1, (j + 1) % 2)
        hidden_hi(FB - 1, 6 * FB - 1)
        for n in range(4):
            if n < 3:
                split_hi(Q_LAST + n + 1, (n + 1) % 2)
            if 1 <= n < 3:
                for t in range(TT):
                    act.wait_ge(bank_free, 24 * FB + 4 * (n - 1) + t + 1)
                    square_sum(t, n - 1, 32 + 4 * (n - 1) + t, t % 2)

        def y_part(t):
            act.wait_ge(rstd_ready, 2 * TT + t + 1)
            act.wait_ge(hg_ready, 2 * TT + t + 1)
            act.activation(hres[:, t, 0:Y_ACT], hres[:, t, 0:Y_ACT], ACT.Copy, scale=rstd[:, t:t + 1]).then_inc(y_act, 1)

        for k, (t, n) in enumerate(LAST):
            act.wait_ge(bank_free, 24 * FB + 8 + k + 1)
            square_sum(t, n, 40 + k, k % 2)
            if k == 3:
                y_part(0)
            if k >= 3 and n == 3:
                y_part(t)

    @block.vector
    def _(dve):
        setups = [0]

        def step(ins):
            setups[0] += 1
            ins.then_inc(setup_step, 1)
            dve.wait_ge(setup_step, setups[0])

        def split_lo(q, slot, n=QC * NW):
            dve.wait_ge(hi_done, q + 1)
            dve.tensor_tensor(wlo[:, slot, 0:n], raw[:, slot, 0:n], whi[:, slot, 0:n].bitcast(F32), ALU.subtract)\
               .then_inc(lo_done, 1)

        def split_half_lo(q, slot, half):
            dve.wait_ge(hi_done, q + 1)
            cols = slice(QC * NW // 2 * half, QC * NW // 2 * (half + 1))
            ins = dve.tensor_tensor(wlo[:, slot, cols], raw[:, slot, cols], whi[:, slot, cols].bitcast(F32), ALU.subtract)
            if half:
                ins.then_inc(lo_done, 1)

        def mean_square(r, t, count):
            dve.wait_ge(sq_sum, count)
            dve.tensor_reduce(ms[:, t:t + 1], ss[:, t, :], AX.X, ALU.add).then_inc(ms_step, 1)
            dve.wait_ge(ms_step, TT * r + t + 1)
            dve.tensor_scalar(ms[:, t:t + 1], ms[:, t:t + 1], 1.0 / DM, EPS, ALU.mult, ALU.add).then_inc(ms_ready, 1)

        def make_diag(r, t):
            dve.wait_ge(rstd_ready, TT * r + t + 1)
            if r:
                dve.wait_ge(rb_done, r)
            dve.tensor_scalar(diag[:, t, :], ident[:, :], rstd[:, t:t + 1], None, ALU.mult).then_inc(diag_ready, 1)

        def u_split_lo(r, ft):
            g = (R_ATTN, R_FFN)[r] + ft
            dve.wait_ge(u_hi, KT * r + ft + 1)
            to = (ft, (8 + ft) % KT)[r]
            dve.scalar_tensor_tensor(out=alo[:, to, :], in0=psB[:, ft % 4, :], scalar=pc[:, g:g + 1],
                                     in1=ahi[:, to, :].bitcast(F32), op0=ALU.mult, op1=ALU.subtract).then_inc(u_lo, 1)

        def spread_rstd(r):
            dve.wait_ge(rb_done, r + 1)
            dve.tensor_copy(rB[:, :], psB[:, 0, :]).then_inc(rb_ready, 1)

        dve.wait_ge(rows_turned, 3)
        dve.tensor_copy(pc[:, :], psA[:, 0, 0:R_ALL]).then_inc(cols_ready, 1)
        dve.tensor_copy(cw[:, :, :], psA[:, 0, 64:64 + 4 * FT].rearrange("p (a f) -> p a f", a=4)).then_inc(cols_ready, 1)
        dve.wait_ge(cols_ready, 2)
        for ft in range(KT):
            u_split_lo(0, ft)
            if ft == 0:
                split_lo(0, 0, QC * SMALL)
            if ft == 3:
                split_lo(1, 1, QC * SMALL)
            if ft in (8, 12):
                split_lo(ft // 4, ft // 4 % 2, QC * SMALL)
        split_lo(4, 0)
        for t in range(TT):
            mean_square(0, t, 12 + t + 1)
        for t in range(TT):
            make_diag(0, t)

        def gla_prep(h, k):
            kh, qh = kq[:, h, :], kq[:, 4 + h, :]
            if k == 0:
                dve.wait_ge(z_abs, h + 1)
                if h >= 1:
                    dve.wait_ge(e_neg, h)
                dve.tensor_scalar(t2[:, :], psB[:, 0, :], pc[:, R_BA + h:R_BA + h + 1], 0.0, ALU.add, ALU.min).then_inc(z_min, 1)
            if k == 1:
                dve.wait_ge(z_min, h + 1)
                dve.wait_ge(z_ln, h + 1)
                dve.tensor_tensor(t2[:, :], t2[:, :], t1[:, :], ALU.subtract).then_inc(z_la, 1)
                dve.wait_ge(z_la, h + 1)
                dve.tensor_tensor_scan(bc[:, :], keep[:, :], t2[:, :], 0.0, ALU.mult, ALU.add).then_inc(bcum, 1)
            if k == 2:
                dve.wait_ge(bcum, h + 1)
                if h >= 1:
                    dve.wait_ge(kd_turned, h)
                b3 = bc[:, :].rearrange("p (n c) -> p n c", c=CH)
                dve.tensor_tensor(t3[:, :].rearrange("p (n c) -> p n c", c=CH),
                                  b3[:, :, CH - 1:CH].broadcast_to([P, NCH, CH]), b3, ALU.subtract).then_inc(to_last, 1)
            if k == 3:
                dve.wait_ge(e_pos, h + 1)
                dve.scalar_tensor_tensor(out=qh, in0=qh, scalar=DK ** -0.5, in1=t1[:, :], op0=ALU.mult, op1=ALU.mult).then_inc(q_e, 1)
                dve.wait_ge(e_last, h + 1)
                dve.tensor_tensor(t3[:, :], t3[:, :], kh, ALU.mult).then_inc(k_d, 1)
                dve.wait_ge(e_neg, h + 1)
                dve.tensor_tensor(kh, kh, t2[:, :], ALU.mult).then_inc(k_e, 1)

        def gla_scores(m):
            dve.wait_ge(st_done, m + 1)
            if m >= 2:
                dve.wait_ge(gla_mm, m - 1)
            dve.copy_predicated(sT[:, m % 2, :], gla_mask[:, :].bitcast(U32), psB[:, 1, 0:P])\
               .then_inc(st_ready, 1)

        def gla_state(h, n):
            if n == 7:
                return
            kv = psB[:, 3, 0:DV]
            new = S[:, (n + 1) % 2, :]
            dve.wait_ge(kv_done, 7 * h + n + 1)
            if n == 0:
                if h >= 1:
                    dve.wait_ge(o_done, TT * h)
                dve.tensor_copy(new, kv).then_inc(s_ready, 1)
            else:
                dve.wait_ge(e_dec, h + 1)
                dve.wait_ge(s_ready, 7 * h + n)
                dve.scalar_tensor_tensor(out=new, in0=S[:, n % 2, :], scalar=dec[:, h % 2, n:n + 1], in1=kv,
                                         op0=ALU.mult, op1=ALU.add).then_inc(s_ready, 1)

        def gla_ms(m):
            dve.wait_ge(o_sq, m + 1)
            if m >= 2:
                dve.wait_ge(o_rstd, m - 1)
            dve.tensor_scalar(g_ms[:, m % 2:m % 2 + 1], g_ss[:, m % 2:m % 2 + 1], 1.0 / DV, EPS, ALU.mult, ALU.add).then_inc(o_ms, 1)

        def gla_out(m):
            h, c = m // TT, m % TT
            dve.wait_ge(o_turned, m + 1)
            for j in range(2):
                ins = dve.tensor_scalar(v[:, c, DV * h + P * j:DV * h + P * j + P], psB[:, 0, P * j:P * j + P],
                                        pc[:, R_GN + j:R_GN + j + 1], None, ALU.mult)
            ins.then_inc(o_ready, 1)

        rope_steps = [0]

        def rope(src, part):
            if part == 0:
                for a in range(0, P, 64):
                    dve.tensor_tensor(rtmp[a:a + 32, :], src[a + 32:a + 64, :], sinT[a + 32:a + 64, :], ALU.mult)
                    ins = dve.tensor_tensor(rtmp[a + 32:a + 64, :], src[a:a + 32, :], sinT[a:a + 32, :], ALU.mult)
                rope_steps[0] += 1
                ins.then_inc(rope_step, 1)
                dve.wait_ge(rope_step, rope_steps[0])
            else:
                rope_steps[0] += 1
                dve.tensor_tensor(src, src, cosT[:, :], ALU.mult).then_inc(rope_step, 1)
                dve.wait_ge(rope_step, rope_steps[0])
                return dve.tensor_tensor(src, src, rtmp[:, :], ALU.add)

        def swa_k_lo():
            dve.wait_ge(k_hi, 1)
            dve.tensor_tensor(kk_lo[:, :, :], kdup[:, :, :], kk_hi[:, :, :].bitcast(F32), ALU.subtract).then_inc(k_lo, 1)

        def swa_max(u):
            i, n, tile = unit_of(u)
            c0 = 0 if n else WIN
            k = s_small[:, u % 3, :, :]
            dve.wait_ge(sc_done, u + 1)
            if u >= 3:
                dve.wait_ge(p_turned, u - 2)
            for e in range(2):
                dve.tensor_tensor_reduce(out=prob[:, u % 3, e, c0:], in0=psB[:, e, c0:256],
                                         in1=swa_mask[:, c0:], scale=1.0, scalar=-3e38, op0=ALU.add, op1=ALU.max,
                                         accum_out=k[:, 0, e:e + 1]).then_inc(mx_done, 1)
            dve.wait_ge(mx_done, 2 * u + 2)
            hs = slice(2 * tile, 2 * tile + 2)
            dve.scalar_tensor_tensor(out=k[:, 1, :], in0=k[:, 0, :], scalar=-HD ** -0.5, in1=nsink[:, hs],
                                     op0=ALU.mult, op1=ALU.min).then_inc(negm, 1)
            dve.wait_ge(negm, u + 1)
            dve.tensor_tensor(k[:, 2, :], sink_b[:, hs], k[:, 1, :], ALU.add).then_inc(sinkm, 1)

        def swa_norm(u):
            c0 = 0 if unit_of(u)[1] else WIN
            k = s_small[:, u % 3, :, :]
            dve.wait_ge(p_exp, 2 * u + 2)
            dve.wait_ge(sink_exp, u + 1)
            dve.tensor_tensor(k[:, 3, :], k[:, 3, :], k[:, 2, :], ALU.add).then_inc(den, 1)
            dve.wait_ge(den, u + 1)
            dve.reciprocal(k[:, 4, :], k[:, 3, :]).then_inc(rden, 1)
            dve.wait_ge(rden, u + 1)
            for e in range(2):
                ins = dve.tensor_scalar(prob[:, u % 3, e, c0:], prob[:, u % 3, e, c0:], k[:, 4, e:e + 1], None, ALU.mult)
            ins.then_inc(p_ready, 1)

        def extras(s):
            m = s - S_GLA
            if 0 <= m < 8 * GH:
                gla_state(m // 8, m % 8)
            if -1 <= m < 8 * GH - 1 and m % 2 == 1:
                gla_scores((m + 1) // 2)
            if 0 <= m < 8 * GH and m % 2 == 1:
                gla_ms(m // 2)
            if 0 <= m - 2 < 8 * GH and m % 2 == 1:
                gla_out((m - 2) // 2)
            if 0 <= s - S_SWA < UNITS:
                swa_max(s - S_SWA)
            for h in range(GH):
                if 0 <= s - (S_PREP + 8 * h) < 8:
                    gla_prep(h, s - (S_PREP + 8 * h))
            k = s - S_KROPE
            if k == 0:
                dve.wait_ge(proj_free, 1)
                dve.wait_ge(trig_ready, 2)
                rope(kraw[:, :], 0)
            if k == 1:
                ins = rope(kraw[:, :], 1)
                rope_steps[0] += 1
                ins.then_inc(rope_step, 1)
                dve.wait_ge(rope_step, rope_steps[0])
                for i in range(KVH):
                    for a in range(0, P, HD):
                        ins = dve.tensor_copy(kdup[a:a + HD, i, :], kraw[HD * i:HD * i + HD, :])
                ins.then_inc(k_ready, 1)
            for g in range(2):
                k = s - S_QROPE[g]
                if 0 <= k < 8:
                    f = 4 * g + k // 2
                    if k == 0:
                        dve.wait_ge(proj_free, pf_after(4 + g + 1))
                    if k % 2 == 0:
                        if f:
                            dve.wait_ge(q_ready, f)
                        rope(sq[:, f, :], 0)
                    else:
                        rope(sq[:, f, :], 1).then_inc(q_ready, 1)

        for m in range(2):
            proj_full(dve, 0, (1, 3)[m])
            both = psA[:, 1 + m, 0:2 * (RANK + P)].rearrange("p (t n) -> p t n", t=2)
            r = rstd[:, 2 * m:2 * m + 2].rearrange("p (t o) -> p t o", o=1)
            dve.tensor_tensor(atok[:, 2 * m:2 * m + 2, :], both[:, :, 0:RANK], r.broadcast_to([P, 2, RANK]), ALU.mult).then_inc(a_ready, 1)
            dve.tensor_tensor(sv[:, 2 * m:2 * m + 2, :], both[:, :, RANK:], r.broadcast_to([P, 2, P]), ALU.mult).then_inc(proj_free, 1)
        spread_rstd(0)
        proj_full(dve, 0, 0)
        dve.wait_ge(rb_ready, 1)
        dve.tensor_tensor(kraw[:, :], psA[:, 0, :], rB[:, :], ALU.mult).then_inc(proj_free, 1)
        split_lo(5, 1)
        dve.wait_ge(a_turned, 1)
        dve.tensor_copy(alow[:, :], psB[0:RANK, 1, :]).then_inc(alow_ready, 1)
        dve.wait_ge(small_loaded, 64)
        step(dve.tensor_scalar(ang[:, :], posb[:, :], trig_sb[:, 0:1], None, ALU.mult))
        step(dve.tensor_scalar(turns[:, :], ang[:, :], 1.0 / TWO_PI, MAGIC, ALU.mult, ALU.add))
        step(dve.tensor_scalar(turns[:, :], turns[:, :], -MAGIC, None, ALU.add))
        for part in (TP1, TP2, TP3):
            step(dve.scalar_tensor_tensor(out=ang[:, :], in0=turns[:, :], scalar=-part, in1=ang[:, :],
                                          op0=ALU.mult, op1=ALU.add))
        dve.tensor_scalar(ang[:, :], ang[:, :], PI_IN, -PI_IN, ALU.min, ALU.max).then_inc(sin_in, 1)
        dve.tensor_scalar(nsink[:, :], sink_b[:, :], -1.0, None, ALU.mult).then_inc(trig_ready, 1)
        dve.wait_ge(sin_out, 2)
        step(dve.scalar_tensor_tensor(out=cosT[:, :], in0=cosT[:, :], scalar=-2.0, in1=cosT[:, :],
                                      op0=ALU.mult, op1=ALU.mult))
        dve.tensor_scalar(cosT[:, :], cosT[:, :], 1.0, None, ALU.add).then_inc(trig_ready, 1)
        with dve.Fori(0, 2) as i:
            for j in range(1, 4):
                split_lo(Q_KQ + 1 + 4 * i + j, (j + 1) % 2)
            for f in range(4):
                proj_full(dve, i + 1, f)
                dve.tensor_tensor(kq[:, bass.ds(4 * i + f, 1), :].rearrange("p a s -> p (a s)"), psA[:, f, :], rB[:, :],
                                  ALU.mult).then_inc(proj_free, 1)
            split_lo(Q_KQ + 5 + 4 * i, 1)

        def gate_scale(g, f):
            proj_full(dve, 7 + g, f)
            if g:
                dve.wait_ge(gla_mixed, f + 1)
            else:
                dve.wait_ge(o_turned, GH * TT)
            dve.tensor_tensor(gsil[:, f, :], psA[:, f, :], rB[:, :], ALU.mult).then_inc(g_scaled, 1)

        def mix_gate(f):
            dve.wait_ge(gate_silu, f + 1)
            tile = v[:, :, P * f:P * f + P]
            dve.tensor_tensor(tile, tile, gsil[:, f % 4, :].rearrange("p (t c) -> p t c", t=TT), ALU.mult).then_inc(gla_mixed, 1)

        def evacuate(n, kind, f0, f1):
            for f in range(f0, f1):
                if kind == "sq":
                    proj_full(dve, 3 + n, f)
                    dve.tensor_tensor(sq[:, 4 * (n - 2) + f, :], psA[:, f, :], rB[:, :], ALU.mult).then_inc(proj_free, 1)
                elif n == 4:
                    gate_scale(0, f)

        for n, (_, kind) in enumerate(groups):
            for j in range(4):
                q = Q_REST + 4 * n + j
                for s in range(4 * q, 4 * q + 4):
                    last = s == 4 * Q_REST + 16 * n + 15
                    if last:
                        evacuate(n, kind, 0, 3)
                    if 0 <= s - S_SWA - 1 < UNITS:
                        swa_norm(s - S_SWA - 1)
                    if s == S_SWA - 1:
                        swa_k_lo()
                    if Q_REST < q < Q_OUT - 1:
                        if q < S_SWA // 4 and s == 4 * q:
                            split_lo(q + 1, (j + 1) % 2)
                        if q >= S_SWA // 4 and s - 4 * q in (1, 2):
                            split_half_lo(q + 1, (j + 1) % 2, s - 4 * q - 1)
                    extras(s)
                    if last:
                        evacuate(n, kind, 3, 4)

        split_lo(Q_OUT, 0)
        for f in range(4):
            mix_gate(f)

        def mix_tile(m):
            kt = (8 + m) % KT
            dve.wait_ge(mix_hi, m + 1)
            if kt >= 8:
                dve.tensor_tensor(alo[:, kt, :], sq[:, kt - 8, :], ahi[:, kt, :].bitcast(F32), ALU.subtract).then_inc(mix_lo, 1)
            else:
                dve.tensor_tensor(alo[:, kt, :].rearrange("p (t c) -> p t c", t=TT), v[:, :, P * kt:P * kt + P],
                                  ahi[:, kt, :].bitcast(F32).rearrange("p (t c) -> p t c", t=TT), ALU.subtract).then_inc(mix_lo, 1)

        mix_tile(0)
        mix_tile(1)
        gate_scale(1, 0)
        gate_scale(1, 1)
        mix_tile(2)
        gate_scale(1, 2)
        gate_scale(1, 3)
        mix_tile(3)
        split_lo(Q_OUT + 1, 1)
        for m in range(4, KT):
            if m < 8:
                mix_gate(m)
            mix_tile(m)
            if m % 4 == 3:
                split_lo(Q_OUT + m // 4 + 1, (m // 4 + 1) % 2)

        def add_h(t, col, g, q_last, b):
            bank_full(dve, g, t, q_last)
            dve.tensor_tensor(hres[:, t, col], hres[:, t, col], ps[b][:, t, :], ALU.add).then_inc(bank_free, 1)

        def add_group(n):
            for t in range(TT):
                dve.wait_ge(x_back[t], 16)
                add_h(t, bass.ts(n, NW), n, Q_OUT + 4 * n + 3, 1)

        add_group(0)
        with dve.Fori(1, 3) as n:
            for j in range(4):
                split_lo(Q_OUT + 1 + 4 * n + j, (j + 1) % 2)
            add_group(n)
        for ft in range(12):
            u_split_lo(1, ft)
            if ft % 3 == 1:
                split_lo(Q_OUT + 13 + ft // 3, (1 + ft // 3) % 2)
        for t in range(TT):
            add_h(t, slice(3 * NW, DM), 3, Q_OUT + 15, 0)
        split_lo(Q_FFN + 1, 1)
        for ft in range(12, KT):
            u_split_lo(1, ft)
        for t in range(TT):
            mean_square(1, t, 16 + 12 + t + 1)
        split_lo(Q_FFN + 2, 0)
        for t in range(TT):
            make_diag(1, t)
        spread_rstd(1)
        split_lo(Q_FFN + 3, 1)

        def gate_evac(b, g, q_last):
            def scale(j):
                bank_full(dve, g, j, q_last)
                if not isinstance(b, int) or j >= 2:
                    dve.wait_ge(conv_done, 4 * b + j - 1)
                dve.tensor_tensor(gate[:, j % 2, :], psA[:, j, :], rB[:, :], ALU.mult).then_inc(bank_free, 1)

            scale(0)
            for j in range(4):
                if j < 3:
                    scale(j + 1)
                tap = bass.ds(4 * b + j, 1)
                dve.wait_ge(conv_in, 4 * b + j + 1)
                dve.scalar_tensor_tensor(out=conv[:, j % 2, 1:], in0=gate[:, j % 2, 0:SEQ - 1], scalar=cw[:, 1, tap],
                                         in1=conv[:, j % 2, 1:], op0=ALU.mult, op1=ALU.add).then_inc(conv_mid, 1)
                dve.wait_ge(conv_mid, 4 * b + j + 1)
                dve.scalar_tensor_tensor(out=conv[:, j % 2, 2:], in0=gate[:, j % 2, 0:SEQ - 2], scalar=cw[:, 0, tap],
                                         in1=conv[:, j % 2, 2:], op0=ALU.mult, op1=ALU.add).then_inc(conv_done, 1)

        def up_evac(b, g, q_last):
            def low(j):
                dve.wait_ge(h_hi, 4 * b + j + 1)
                dve.tensor_tensor(hT_lo[:, j, :], sg[:, j, :], hT_hi[:, j, :].bitcast(F32), ALU.subtract).then_inc(h_lo, 1)
            for j in range(4):
                bank_full(dve, g, j, q_last)
                dve.wait_ge(silu_scaled, 4 * b + j + 1)
                dve.tensor_tensor(sg[:, j, :], sg[:, j, :], psB[:, j, :], ALU.mult).then_inc(bank_free, 1)
                if j >= 1:
                    low(j - 1)
            low(3)

        def down_evac(n, g, q_last, b):
            for t in range(TT):
                add_h(t, slice(NW * n, NW * n + NW), g, q_last, b)

        split_lo(Q_FFN + 4, 0)
        split_lo(Q_FFN + 5, 1)
        gate_evac(0, 4, Q_FFN + 3)
        for j in range(2, 4):
            split_lo(Q_FFN + 4 + j, j % 2)
        split_lo(Q_LOOP, 0)
        with dve.Fori(1, FB) as b:
            q0 = Q_LOOP - 12 + 12 * b
            g0 = 6 * b
            split_lo(q0 + 1, 1)
            up_evac(b - 1, g0 - 1, q0 - 1)
            for j in range(1, 4):
                split_lo(q0 + j + 1, (j + 1) % 2)
            split_lo(q0 + 5, 1)
            gate_evac(b, g0, q0 + 3)
            for n in range(4):
                split_lo(q0 + 6 + n, n % 2)
                down_evac(n, g0 + 1 + n, q0 + 4 + n, 1 - n % 2)
            for j in range(9, 12):
                split_lo(q0 + j + 1, (j + 1) % 2)
        up_evac(FB - 1, 6 * FB - 1, Q_LAST - 1)
        for n in range(4):
            if n < 3:
                split_lo(Q_LAST + n + 1, (n + 1) % 2)
            if n < 2:
                down_evac(n, 6 * FB + n, Q_LAST + n, n % 2)

        def y_part(t):
            dve.wait_ge(rstd_ready, 2 * TT + t + 1)
            dve.wait_ge(hg_ready, 2 * TT + t + 1)
            dve.tensor_scalar(hres[:, t, Y_ACT:3 * NW], hres[:, t, Y_ACT:3 * NW], rstd[:, t:t + 1], None, ALU.mult)\
               .then_inc(y_ready, 1)
            dve.scalar_tensor_tensor(out=hres[:, t, 3 * NW:], in0=hres[:, t, 3 * NW:], scalar=rstd[:, t:t + 1],
                                     in1=fgain[:, 3 * NW:], op0=ALU.mult, op1=ALU.mult).then_inc(y_ready, 1)

        dve.wait_ge(gain_loaded, 16)
        for k, (t, n) in enumerate(LAST):
            col = slice(NW * n, NW * n + NW)
            dve.wait_ge(last_done, k + 1)
            dve.tensor_tensor(hres[:, t, col], hres[:, t, col], ps[n % 2][:, t, :], ALU.add).then_inc(bank_free, 1)
            if k == 3:
                mean_square(2, 0, 40 + k)
            if n == 3 and k >= 3:
                mean_square(2, t, 40 + k + 1)
            if k == 3:
                y_part(0)
            if n == 3 and k >= 3:
                y_part(t)

    @block.tensor
    def _(pe):
        def three(dst, a, b, first, last):
            pe.matmul(dst, a[0], b[0], start=first, stop=False, skip_group_check=True)
            pe.matmul(dst, a[0], b[1], start=False, stop=False, skip_group_check=True)
            return pe.matmul(dst, a[1], b[0], start=False, stop=last, skip_group_check=True)

        def weights(slot, c, a, n, width=NW):
            return tuple(quad(w, slot, width)[:, c, a:a + n] for w in (whi, wlo))

        def acts(k, a=0, n=SEQ):
            return ahi[:, k, a:a + n], alo[:, k, a:a + n]

        def feature_major(bank, slot, c, k, first, last):
            for f in range(4):
                yield f, lambda f=f: three(bank[:, f, :], weights(slot, c, P * f, P), acts(k), first, last)

        def token_major(bank, slot, c, lhs, first, last):
            for t in range(TT):
                yield t, lambda t=t: three(bank[:, t, :], lhs(t), weights(slot, c, 0, NW), first, last)

        def turn_u(r, ft):
            if ft >= 4:
                pe.wait_ge(u_lo, KT * r + ft - 3)
            if r == 0 and ft % 4 == 0:
                pe.wait_ge(x_loaded[ft // 4], 16)
            for t in range(TT):
                ins = pe.transpose(psB[:, ft % 4, P * t:P * t + P], hres[:, t, P * ft:P * ft + P], ident[:, :])
            ins.then_inc(u_turned, 1)

        def spread_rstd(r):
            pe.wait_ge(u_lo, KT * r + KT)
            pe.wait_ge(diag_ready, TT * r + TT)
            for t in range(TT):
                ins = pe.matmul(psB[:, 0, P * t:P * t + P], ones[:, :], diag[:, t, :], start=True, stop=True)
            ins.then_inc(rb_done, 1)

        pe.wait_ge(ident_ready, 2)
        for ft in range(2):
            turn_u(0, ft)
        pe.wait_ge(rows_loaded, 16 * 8)
        pe.transpose(psA[:, 0, 0:R_ALL], prow[0:R_ALL, 0, :], ident[0:R_ALL, 0:R_ALL]).then_inc(rows_turned, 1)
        for m in range(2):
            pe.transpose(psA[:, 0, 64 + 88 * m:64 + 88 * m + 88], prow[0:88, 1 + m, :], ident[0:88, 0:88]).then_inc(rows_turned, 1)

        for ft in range(2, 4):
            turn_u(0, ft)
        pe.wait_ge(cols_ready, 2)
        for k in range(KT):
            q, c = k // QC, k % QC
            if c == 0:
                pe.wait_ge(lo_done, q + 1)
            pe.wait_ge(u_lo, k + 1)
            first, last = k == 0, k == KT - 1
            ins = three(psA[:, 0, :], weights(q % 2, c, 0, P, SMALL), acts(k), first, last)
            if last:
                ins.then_inc(proj_done, 1)
            for t in range(TT):
                n = (RANK + P) * (t % 2)
                ins = three(psA[:, 1 + t // 2, n:n + RANK + P], acts(k, P * t, P), weights(q % 2, c, P, RANK + P, SMALL),
                            first and t % 2 == 0, last)
                if last and t == 1:
                    ins.then_inc(proj_done, 1)
            if c == QC - 1:
                ins.then_inc(quad_used, 1)
            if k + 4 < KT:
                turn_u(0, k + 4)
        spread_rstd(0)
        pe.wait_ge(a_ready, 2)
        for t in range(TT):
            ins = pe.matmul(psB[0:RANK, 1, P * t:P * t + P], atok[:, t, :], ident[:, :], start=True, stop=True)
        ins.then_inc(a_turned, 1)

        def group(q0, bank, kind, done, free=None, extras=None, ready=None, kts=range(KT)):
            for j in range(4):
                pe.wait_ge(lo_done, q0 + j + 1)
                for c in range(QC):
                    n = QC * j + c
                    k, first, last = kts[n], n == 0, n == KT - 1
                    if ready:
                        ready(n)
                    for f in range(4):
                        if first and free:
                            free(f)
                        if kind == "token":
                            ins = three(bank[:, f, :], acts(k, P * f, P), weights(j % 2, c, 0, NW), first, last)
                        else:
                            ins = three(bank[:, f, :], weights(j % 2, c, P * f, P), acts(k), first, last)
                        if last and f < 3:
                            ins.then_inc(done, 1)
                    if c == QC - 1:
                        ins.then_inc(quad_used, 1)
                    if extras:
                        extras(4 * (q0 + j) + c)

        def turns_before(s):
            return max(0, (s - (S_GLA + 3) + 1) // 2)

        def gla_prep(h, k, s):
            if k == 0:
                if h == 0:
                    pe.wait_ge(rb_ready, 1)
                    pe.wait_ge(alow_ready, 1)
                else:
                    pe.wait_ge(kd_ready, h)
                    if turns_before(s):
                        pe.wait_ge(o_ready, turns_before(s))
                pe.matmul(psB[:, 0, :], wau[:, DK * h:DK * h + DK], alow[:, :], start=True, stop=True).then_inc(z_done, 1)
            if k == 4:
                pe.wait_ge(k_d, h + 1)
                if turns_before(s):
                    pe.wait_ge(o_ready, turns_before(s))
                for t in range(TT):
                    ins = pe.transpose(psB[:, 0, DK * t:DK * t + DK], t3[:, P * t:P * t + P], ident[:, :])
                ins.then_inc(kd_turned, 1)

        def gla_scores(m):
            h, c = m // TT, m % TT
            pe.wait_ge(k_e, h + 1)
            pe.wait_ge(q_e, h + 1)
            if m == 0:
                pe.wait_ge(masks_ready, 4)
            if m >= 1:
                pe.wait_ge(st_ready, m)
            pe.matmul(psB[:, 1, 0:P], kq[:, h, P * c:P * c + P], kq[:, 4 + h, P * c:P * c + P],
                      start=True, stop=True).then_inc(st_done, 1)

        def gla_step(h, n):
            c, b, m = n // 2, n % 2, TT * h + n // 2
            vt = v[:, c, DV * h:DV * h + DV]
            o = psB[:, 2, 0:DV]
            if b == 0:
                pe.wait_ge(st_ready, m + 1)
                if m >= 1:
                    pe.wait_ge(o_norm, m)
                ins = pe.matmul(o, sT[:, m % 2, :], vt, start=True, stop=False, skip_group_check=True)
            if n >= 1:
                pe.wait_ge(s_ready, 7 * h + n)
                ins = pe.matmul(o[CH * b:CH * b + CH, :], kq[:, 4 + h, CH * n:CH * n + CH], S[:, n % 2, :],
                                start=False, stop=True, skip_group_check=True)
            if b == 0:
                ins.then_inc(gla_mm, 1)
            else:
                ins.then_inc(o_done, 1)
            if n < 7:
                pe.wait_ge(kd_ready, h + 1)
                if h + n:
                    pe.wait_ge(s_ready, 7 * h + n)
                rows = slice(CH * b, CH * b + CH)
                pe.matmul(psB[:, 3, 0:DV], kdT[rows, h % 2, c, :], v[rows, c, DV * h:DV * h + DV],
                          start=True, stop=True).then_inc(kv_done, 1)

        def gla_turn(m, s):
            pe.wait_ge(o_norm, m + 1)
            pe.wait_ge(z_min, min(GH, (s - S_PREP) // 8 + 1))
            pe.wait_ge(kd_ready, min(GH, (s - S_PREP - 4) // 8 + 1))
            if m >= 1:
                pe.wait_ge(o_ready, m)
            for j in range(2):
                ins = pe.transpose(psB[:, 0, P * j:P * j + P], on[:, m % 2, P * j:P * j + P], ident[:, :])
            ins.then_inc(o_turned, 1)

        def swa_scores(u):
            i, n, tile = unit_of(u)
            a = P * (n - 1) if n else 0
            c0 = 0 if n else WIN
            pe.wait_ge(k_lo, 1)
            pe.wait_ge(q_lo, u + 1)
            if u == 0:
                pe.wait_ge(kd_ready, GH)
                pe.wait_ge(o_ready, GH * TT)
            if u >= 1:
                pe.wait_ge(mx_done, 2 * u)
            for e in range(2):
                rows = slice(HD * e, HD * e + HD)
                pe.matmul(psB[:, e, c0:256], qs[:, u % 3, e, :], kk_hi[:, i, a:P * n + P],
                          start=True, stop=False, skip_group_check=True)
                ins = pe.matmul(psB[:, e, c0:256], qs[rows, u % 3, e, :], kk_lo[rows, i, a:P * n + P],
                                start=False, stop=True, skip_group_check=True)
            ins.then_inc(sc_done, 1)

        def swa_turn(u):
            a = 0 if unit_of(u)[1] else 1
            pe.wait_ge(p_ready, u + 1)
            if u >= 1:
                pe.wait_ge(pT_ready, u)
            for kt in range(a, 2):
                for e in range(2):
                    ins = pe.transpose(psB[:, 2, P * (2 * kt + e):P * (2 * kt + e) + P], prob[:, u % 3, e, P * kt:P * kt + P],
                                       ident[:, :])
            ins.then_inc(p_turned, 1)

        def swa_pv(u):
            i, n, _ = unit_of(u)
            a = 0 if n else 1
            pe.wait_ge(pT_ready, u + 1)
            if u >= 1:
                pe.wait_ge(so_ready, u)
            for e in range(2):
                for kt in range(a, 2):
                    ins = pe.matmul(psB[HD * e:HD * e + HD, 3, 0:P],
                                    sv[:, n - 1 + kt, HD * i:HD * i + HD], pT[:, u % 2, 2 * kt + e, :],
                                    start=(kt == a), stop=(kt == 1))
            ins.then_inc(pv_done, 1)

        def extras(s):
            for h in range(GH):
                if 0 <= s - (S_PREP + 8 * h) < 8:
                    gla_prep(h, s - (S_PREP + 8 * h), s)
            m = s - S_GLA
            if 0 <= m < 8 * GH:
                gla_step(m // 8, m % 8)
            if -1 <= m < 8 * GH - 1 and m % 2 == 1:
                gla_scores((m + 1) // 2)
            if 0 <= m - 2 < 8 * GH and m % 2 == 1:
                gla_turn((m - 2) // 2, s)
            u = s - S_SWA
            if 0 <= u < UNITS:
                swa_scores(u)
            if 0 <= u - 2 < UNITS:
                swa_turn(u - 2)
            if 0 <= u - 3 < UNITS:
                swa_pv(u - 3)

        with pe.Fori(0, 2) as i:
            group(Q_KQ + 4 * i, psA, "feature", proj_done, free=lambda f: pe.wait_ge(proj_free, i * (f + 1) + 3))
        for n, (_, kind) in enumerate(groups):
            group(Q_REST + 4 * n, psA, "token" if kind == "v" else "feature", proj_done,
                  free=(lambda f: pe.wait_ge(g_scaled, f + 1)) if n == 5 else
                       (lambda f: pe.wait_ge(proj_free, pf_after(1 + n) + f + 1)), extras=extras)

        order = [(8 + n) % KT for n in range(KT)]
        pe.wait_ge(so_ready, UNITS)
        group(Q_OUT, psB, "token", bank_done, ready=lambda k: pe.wait_ge(mix_lo, k + 1), kts=order)
        with pe.Fori(1, 3) as n:
            group(Q_OUT + 4 * n, psB, "token", bank_done, free=lambda f: pe.wait_ge(bank_free, 4 * n + f - 3), kts=order)

        def turn_h(s):
            n = s - 4 * (Q_OUT + 12)
            if n == 0:
                pe.wait_ge(bank_free, 12)
            if n < 12:
                turn_u(1, n)

        pe.wait_ge(g_scaled, 8)
        group(Q_OUT + 12, psA, "token", bank_done, kts=order, extras=turn_h)

        def down(n, q, bank, b, g, free=True):
            pe.wait_ge(lo_done, q + 1)
            for c in range(QC):
                pe.wait_ge(h_lo, 4 * b + c + 1)
                for t in range(TT):
                    if c == 0:
                        pe.wait_ge(bank_free, 4 * (g - 2) + t + 1)
                    ins = three(bank[:, t, :], (hT_hi[:, c, P * t:P * t + P], hT_lo[:, c, P * t:P * t + P]),
                                weights(n % 2, c, 0, NW), c == 0, c == QC - 1)
                    if c == QC - 1 and t < 3:
                        ins.then_inc(bank_done, 1)
            ins.then_inc(quad_used, 1)

        def freed(g):
            return lambda f: pe.wait_ge(bank_free, 4 * (g - 2) + f + 1)

        def last_h(s):
            n = s - 4 * Q_FFN
            if n == 0:
                pe.wait_ge(bank_free, 16)
            if n < 4:
                turn_u(1, 12 + n)
            if n == 9:
                spread_rstd(1)

        group(Q_FFN, psA, "feature", bank_done, free=lambda f: pe.wait_ge(bank_free, 12 + f + 1),
              ready=lambda n: pe.wait_ge(u_lo, KT + n + 1), extras=last_h, kts=order)
        pe.wait_ge(rb_ready, 2)
        group(Q_FFN + 4, psB, "feature", bank_done, kts=order)
        with pe.Fori(1, FB) as b:
            q0 = Q_LOOP - 12 + 12 * b
            g0 = 6 * b
            group(q0, psA, "feature", bank_done, free=freed(g0), kts=order)
            for n in range(4):
                down(n, q0 + 4 + n, ps[1 - n % 2], b - 1, g0 + 1 + n)
            group(q0 + 8, psB, "feature", bank_done, free=freed(g0 + 5), kts=order)
        for n in range(2):
            down(n, Q_LAST + n, ps[n % 2], FB - 1, 6 * FB + n)
        for k, (t, n) in enumerate(LAST):
            pe.wait_ge(lo_done, Q_LAST + n + 1)
            pe.wait_ge(bank_free, 24 * FB + 4 * (n - 2) + t + 1)
            for c in range(QC):
                ins = three(ps[n % 2][:, t, :], (hT_hi[:, c, P * t:P * t + P], hT_lo[:, c, P * t:P * t + P]),
                            weights(n % 2, c, 0, NW), c == 0, c == QC - 1)
            ins.then_inc(last_done, 1)

    ctx.close()


_INS = ["x", "positions", "attn_norm", "w_in", "w_a_up", "b_a_up", "gla_norm", "sinks", "w_out", "ffn_norm",
        "w_gate", "w_up", "conv_w", "conv_b", "w_down", "final_norm"]


def kernel(**inputs):
    import numpy as _np
    import concourse.bacc as _bacc
    from concourse import mybir as _mybir
    from concourse.bass_utils import run_bass_kernel_spmd as _run

    nc = _bacc.Bacc("TRN2", target_bir_lowering=False, num_devices=1)
    arrays, args = {}, []
    for name in _INS:
        a = _np.ascontiguousarray(inputs[name])
        arrays[f"in_{name}"] = a
        args.append(nc.dram_tensor(f"in_{name}", a.shape, _mybir.dt.from_np(a.dtype), kind="ExternalInput").ap())
    half = HD // 2
    part = _np.arange(P)
    freq = (THETA ** (-(part % half).astype(_np.float32) / _np.float32(half))).astype(_np.float32)
    sign = _np.where(part % HD < half, 1.0, -1.0).astype(_np.float32)
    arrays["trig"] = _np.ascontiguousarray(_np.stack([freq, sign], axis=1))
    args.append(nc.dram_tensor("trig", (P, 2), _mybir.dt.float32, kind="ExternalInput").ap())
    args.append(nc.dram_tensor("out", (1, SEQ, DM), _mybir.dt.float32, kind="ExternalOutput").ap())
    build(nc, *args)
    r = _run(nc, [arrays], core_ids=[0])
    return r.results[0]["out"]
```
